# Optimizing a Trainium2 kernel written in Bass

```python
import math
import jax, jax.numpy as jnp
from jax import lax
import numpy as np

D_MODEL = 1024
BATCH = 1
SEQ = 256
DEPTH = 2

N_MIXERS = 2
N_HEADS = 16
HEAD_DIM = D_MODEL // N_HEADS
BLOCK_Q = 128
POOL_WINDOWS = (2, 4, 8, 16)
N_POOL_GROUPS = len(POOL_WINDOWS)
POOL_GROUP = D_MODEL // N_POOL_GROUPS
D_FF = 2816
PLE_DIM = 256
EPS = 1e-6


def rms_norm(x, g):
    xf = x.astype(jnp.float32)
    y = xf * lax.rsqrt(jnp.mean(xf * xf, axis=-1, keepdims=True) + EPS)
    return (y * g.astype(jnp.float32)).astype(x.dtype)

def swiglu(h, w_gu, w_down):
    gate, up = jnp.split(h @ w_gu, 2, axis=-1)
    return (jax.nn.silu(gate) * up) @ w_down

def stick_breaking_attention(h, w_qkv, q_gain, k_gain, w_o):
    B, S, _ = h.shape
    q, k, v = jnp.split(h @ w_qkv, 3, axis=-1)
    q = rms_norm(q.reshape(B, S, N_HEADS, HEAD_DIM), q_gain)
    k = rms_norm(k.reshape(B, S, N_HEADS, HEAD_DIM), k_gain)
    v = v.reshape(B, S, N_HEADS, HEAD_DIM)
    q, k, v = (t.transpose(0, 2, 1, 3) for t in (q, k, v))
    scale = 1.0 / math.sqrt(HEAD_DIM)
    outs = []
    for blk in range(S // BLOCK_Q):
        t0 = blk * BLOCK_Q
        t1 = t0 + BLOCK_Q
        qb = q[:, :, t0:t1]
        kb = k[:, :, :t1]
        vb = v[:, :, :t1]
        z = jnp.einsum('bhqd,bhkd->bhqk', qb, kb).astype(jnp.float32) * scale
        qpos = t0 + jnp.arange(BLOCK_Q)
        kpos = jnp.arange(t1)
        causal = kpos[None, :] < qpos[:, None]
        log_stay = jnp.where(causal, jax.nn.log_sigmoid(-z), 0.0)
        log_after = lax.cumsum(log_stay, axis=3, reverse=True) - log_stay
        weights = jnp.where(causal, jnp.exp(jax.nn.log_sigmoid(z) + log_after), 0.0)
        outs.append(jnp.einsum('bhqk,bhkd->bhqd', weights.astype(vb.dtype), vb))
    o = jnp.concatenate(outs, axis=2)
    o = o.transpose(0, 2, 1, 3).reshape(B, S, D_MODEL)
    return o @ w_o

def multiscale_pool_mixer(h, w_in, w_grp, scale):
    B, S, _ = h.shape
    u = (h @ w_in).reshape(B, S, N_POOL_GROUPS, POOL_GROUP)
    uf = u.astype(jnp.float32)
    c = jnp.cumsum(uf, axis=1)
    pos = jnp.arange(S)
    outs = []
    for gi, w in enumerate(POOL_WINDOWS):
        cg = c[:, :, gi]
        cpad = jnp.pad(cg, ((0, 0), (w, 0), (0, 0)))
        wsum = cpad[:, w:] - cpad[:, :S]
        cnt = jnp.minimum(pos + 1, w).astype(jnp.float32)
        outs.append(wsum / cnt[None, :, None] - uf[:, :, gi])
    pooled = jnp.stack(outs, axis=2).astype(h.dtype)
    y = jnp.einsum('bsgc,gcd->bsgd', pooled, w_grp).reshape(B, S, D_MODEL)
    return y * scale

def first_inputs(seed: int = 0) -> dict:
    key = jax.random.key(seed)
    ks = iter(jax.random.split(key, 32))
    n_a = (DEPTH + 1) // 2
    n_b = DEPTH // 2
    f32 = jnp.float32

    def w(shape, fan_in):
        return jax.random.normal(next(ks), shape, f32) * fan_in ** -0.5

    def gain(shape):
        return 1.0 + 0.05 * jax.random.normal(next(ks), shape, f32)

    return {
        "x": jax.random.normal(next(ks), (BATCH, SEQ, D_MODEL), f32),
        "p": jax.random.normal(next(ks), (DEPTH, BATCH, SEQ, PLE_DIM), f32),
        "norm_ffn1": gain((DEPTH, D_MODEL)),
        "w_ffn1_gu": w((DEPTH, D_MODEL, 2 * D_FF), D_MODEL),
        "w_ffn1_down": w((DEPTH, D_FF, D_MODEL), D_FF),
        "norm_mix": gain((DEPTH, D_MODEL)),
        "w_qkv": w((n_a, D_MODEL, 3 * D_MODEL), D_MODEL),
        "q_norm": gain((n_a, HEAD_DIM)),
        "k_norm": gain((n_a, HEAD_DIM)),
        "w_o": w((n_a, D_MODEL, D_MODEL), D_MODEL),
        "w_pool_in": w((n_b, D_MODEL, D_MODEL), D_MODEL),
        "w_pool_grp": w((n_b, N_POOL_GROUPS, POOL_GROUP, POOL_GROUP), POOL_GROUP),
        "pool_scale": gain((n_b, D_MODEL)),
        "norm_ffn2": gain((DEPTH, D_MODEL)),
        "w_ffn2_gu": w((DEPTH, D_MODEL, 2 * D_FF), D_MODEL),
        "w_ffn2_down": w((DEPTH, D_FF, D_MODEL), D_FF),
        "norm_ple": gain((DEPTH, D_MODEL)),
        "w_ple_gate": w((DEPTH, D_MODEL, D_MODEL), D_MODEL),
        "w_ple_proj": w((DEPTH, PLE_DIM, D_MODEL), PLE_DIM),
    }

def first_block(x, p, norm_ffn1, w_ffn1_gu, w_ffn1_down, norm_mix, w_qkv, q_norm,
              k_norm, w_o, w_pool_in, w_pool_grp, pool_scale, norm_ffn2,
              w_ffn2_gu, w_ffn2_down, norm_ple, w_ple_gate, w_ple_proj):
    for i in range(DEPTH):
        x = x + 0.5 * swiglu(rms_norm(x, norm_ffn1[i]), w_ffn1_gu[i], w_ffn1_down[i])
        h = rms_norm(x, norm_mix[i])
        j = i // N_MIXERS
        if i % N_MIXERS == 0:
            mix = stick_breaking_attention(h, w_qkv[j], q_norm[j], k_norm[j], w_o[j])
        else:
            mix = multiscale_pool_mixer(h, w_pool_in[j], w_pool_grp[j], pool_scale[j])
        x = x + mix
        x = x + 0.5 * swiglu(rms_norm(x, norm_ffn2[i]), w_ffn2_gu[i], w_ffn2_down[i])
        gate = jax.nn.sigmoid(rms_norm(x, norm_ple[i]) @ w_ple_gate[i])
        x = x + gate * (p[i] @ w_ple_proj[i])
    return x


CHUNK = 64
Q_BLOCK = 128
ROPE_THETA = 10000.0
LN_EPS = 1e-5
RMS_EPS = 1e-6
DN_ALPHA = (2 * DEPTH) ** 0.25
DN_BETA = (8 * DEPTH) ** -0.25
N_MLA = (DEPTH + 1) // 2
N_DSA = DEPTH // 2

MLA_HEADS = 8
MLA_NOPE = 128
MLA_ROPE = 64
MLA_V = 128
MLA_Q_RANK = 384
MLA_KV_RANK = 256
MLA_IN = MLA_Q_RANK + MLA_KV_RANK + MLA_ROPE

DSA_HEADS = 8
DSA_HEAD_DIM = D_MODEL // DSA_HEADS
IDX_HEADS = 8
IDX_DIM = 64
DSA_TOPK_MAX = 256
DSA_HD = DSA_HEADS * DSA_HEAD_DIM
DSA_IN = 3 * DSA_HD + IDX_HEADS * IDX_DIM + IDX_DIM + IDX_HEADS

PEER_HEADS = 8
PEER_NKEYS = 128
PEER_EXPERTS = PEER_NKEYS * PEER_NKEYS
PEER_QDIM = 256
PEER_TOPK = 16
PEER_TOK_BLOCK = 128


def _normal(key, shape, scale):
    return jax.random.normal(key, shape, jnp.float32) * scale

def _layernorm(x, g, b):
    xf = x.astype(jnp.float32)
    mu = jnp.mean(xf, axis=-1, keepdims=True)
    var = jnp.mean(jnp.square(xf - mu), axis=-1, keepdims=True)
    return ((xf - mu) * lax.rsqrt(var + LN_EPS) * g + b).astype(x.dtype)

def _rmsnorm(x, g):
    xf = x.astype(jnp.float32)
    ms = jnp.mean(jnp.square(xf), axis=-1, keepdims=True)
    return (xf * lax.rsqrt(ms + RMS_EPS) * g).astype(x.dtype)

def _rope_tables(seq, dim):
    inv = ROPE_THETA ** (-jnp.arange(0, dim, 2, dtype=jnp.float32) / dim)
    ang = jnp.arange(seq, dtype=jnp.float32)[:, None] * inv[None, :]
    return jnp.cos(ang), jnp.sin(ang)

def _apply_rope(x, cos, sin):
    x1, x2 = jnp.split(x.astype(jnp.float32), 2, axis=-1)
    c = cos[:, None, :]
    s = sin[:, None, :]
    return jnp.concatenate([x1 * c - x2 * s, x2 * c + x1 * s], axis=-1).astype(x.dtype)

def _chunk_causal_attention(q, k, v, scale):
    B, S, H, Dq = q.shape
    nqb = S // Q_BLOCK
    qb = q.reshape(B, nqb, Q_BLOCK, H, Dq).transpose(1, 0, 2, 3, 4)
    key_chunk = jnp.arange(S) // CHUNK

    def one_block(args):
        q_blk, blk = args
        q_chunk = (blk * Q_BLOCK + jnp.arange(Q_BLOCK)) // CHUNK
        s = jnp.einsum('bqhd,bkhd->bhqk', q_blk, k).astype(jnp.float32) * scale
        mask = key_chunk[None, :] <= q_chunk[:, None]
        s = jnp.where(mask[None, None], s, -jnp.inf)
        p = jax.nn.softmax(s, axis=-1).astype(v.dtype)
        return jnp.einsum('bhqk,bkhd->bqhd', p, v)

    out = lax.map(one_block, (qb, jnp.arange(nqb)))
    return out.transpose(1, 0, 2, 3, 4).reshape(B, S, H, v.shape[-1])

def _mla_mixer(x, w_in, q_norm, kv_norm, w_uq, w_ukv, w_o):
    B, S, _ = x.shape
    cos, sin = _rope_tables(S, MLA_ROPE)
    h = x @ w_in
    cq, ckv, k_rope = jnp.split(h, [MLA_Q_RANK, MLA_Q_RANK + MLA_KV_RANK], axis=-1)
    q = jnp.einsum('bsr,rhd->bshd', _rmsnorm(cq, q_norm), w_uq)
    kv = jnp.einsum('bsr,rhd->bshd', _rmsnorm(ckv, kv_norm), w_ukv)
    q_nope, q_rope = jnp.split(q, [MLA_NOPE], axis=-1)
    k_nope, v = jnp.split(kv, [MLA_NOPE], axis=-1)
    q_rope = _apply_rope(q_rope, cos, sin)
    k_rope = _apply_rope(k_rope[:, :, None, :], cos, sin)
    q = jnp.concatenate([q_nope, q_rope], axis=-1)
    k = jnp.concatenate([k_nope, jnp.broadcast_to(k_rope, (B, S, MLA_HEADS, MLA_ROPE))], axis=-1)
    o = _chunk_causal_attention(q, k, v, (MLA_NOPE + MLA_ROPE) ** -0.5)
    return o.reshape(B, S, MLA_HEADS * MLA_V) @ w_o

def _dsa_mixer(x, w_in, w_o):
    B, S, _ = x.shape
    cos_h, sin_h = _rope_tables(S, DSA_HEAD_DIM)
    cos_i, sin_i = _rope_tables(S, IDX_DIM)
    h = x @ w_in
    o1 = 3 * DSA_HD + IDX_HEADS * IDX_DIM
    q, k, v, q_idx, k_idx, w_idx = jnp.split(
        h, [DSA_HD, 2 * DSA_HD, 3 * DSA_HD, o1, o1 + IDX_DIM], axis=-1)
    q = _apply_rope(q.reshape(B, S, DSA_HEADS, DSA_HEAD_DIM), cos_h, sin_h)
    k = _apply_rope(k.reshape(B, S, DSA_HEADS, DSA_HEAD_DIM), cos_h, sin_h)
    v = v.reshape(B, S, DSA_HEADS, DSA_HEAD_DIM)
    q_idx = _apply_rope(q_idx.reshape(B, S, IDX_HEADS, IDX_DIM), cos_i, sin_i)
    k_idx = _apply_rope(k_idx[:, :, None, :], cos_i, sin_i)[:, :, 0, :]
    w_idx = w_idx * (IDX_HEADS ** -0.5 * IDX_DIM ** -0.5)
    topk = min(DSA_TOPK_MAX, S // 4)
    nqb = S // Q_BLOCK
    key_chunk = jnp.arange(S) // CHUNK
    scale = DSA_HEAD_DIM ** -0.5

    def per_batch(args):
        q_b, k_b, v_b, qi_b, ki_b, wi_b = args
        qb = q_b.reshape(nqb, Q_BLOCK, DSA_HEADS, DSA_HEAD_DIM)
        qib = qi_b.reshape(nqb, Q_BLOCK, IDX_HEADS, IDX_DIM)
        wib = wi_b.reshape(nqb, Q_BLOCK, IDX_HEADS)

        def per_block(bargs):
            q_blk, qi_blk, wi_blk, blk = bargs
            q_chunk = (blk * Q_BLOCK + jnp.arange(Q_BLOCK)) // CHUNK
            logits = jnp.einsum('qhd,kd->qhk', qi_blk, ki_b).astype(jnp.float32)
            idx_score = jnp.einsum('qh,qhk->qk', wi_blk.astype(jnp.float32), jax.nn.relu(logits))
            admissible = key_chunk[None, :] <= q_chunk[:, None]
            idx_score = jnp.where(admissible, idx_score, -jnp.inf)
            _, sel = lax.top_k(idx_score, topk)
            k_sel = k_b[sel]
            v_sel = v_b[sel]
            valid = key_chunk[sel] <= q_chunk[:, None]
            s = jnp.einsum('qhd,qkhd->qhk', q_blk, k_sel).astype(jnp.float32) * scale
            s = jnp.where(valid[:, None, :], s, -jnp.inf)
            p = jax.nn.softmax(s, axis=-1).astype(v_sel.dtype)
            return jnp.einsum('qhk,qkhd->qhd', p, v_sel)

        ob = lax.map(per_block, (qb, qib, wib, jnp.arange(nqb)))
        return ob.reshape(S, DSA_HD)

    o = lax.map(per_batch, (q, k, v, q_idx, k_idx, w_idx))
    return o @ w_o

def _peer(x, w_q, sub_keys, w_down, w_up):
    B, S, D = x.shape
    T = B * S
    xt = x.reshape(T, D)
    q = (xt @ w_q).reshape(T, PEER_HEADS, 2, PEER_QDIM // 2)
    s1 = jnp.einsum('thd,hnd->thn', q[:, :, 0], sub_keys[0]).astype(jnp.float32)
    s2 = jnp.einsum('thd,hnd->thn', q[:, :, 1], sub_keys[1]).astype(jnp.float32)
    v1, i1 = lax.top_k(s1, PEER_TOPK)
    v2, i2 = lax.top_k(s2, PEER_TOPK)
    cand = (v1[..., :, None] + v2[..., None, :]).reshape(T, PEER_HEADS, PEER_TOPK * PEER_TOPK)
    cand_idx = (i1[..., :, None] * PEER_NKEYS + i2[..., None, :]).reshape(
        T, PEER_HEADS, PEER_TOPK * PEER_TOPK)
    best, pos = lax.top_k(cand, PEER_TOPK)
    expert = jnp.take_along_axis(cand_idx, pos, axis=-1)
    gate = jax.nn.softmax(best, axis=-1)
    n_e = PEER_HEADS * PEER_TOPK
    nb = T // PEER_TOK_BLOCK
    xb = xt.reshape(nb, PEER_TOK_BLOCK, D)
    eb = expert.reshape(nb, PEER_TOK_BLOCK, n_e)
    gb = gate.reshape(nb, PEER_TOK_BLOCK, n_e)

    def per_block(args):
        x_blk, e_blk, g_blk = args
        u = w_down[e_blk]
        a = jnp.einsum('td,ted->te', x_blk, u).astype(jnp.float32)
        hg = (jax.nn.gelu(a, approximate=False) * g_blk).astype(w_up.dtype)
        return jnp.einsum('te,ted->td', hg, w_up[e_blk]).astype(x_blk.dtype)

    y = lax.map(per_block, (xb, eb, gb))
    return y.reshape(B, S, D)

def second_inputs(seed: int = 0) -> dict:
    key = jax.random.key(seed)
    ks = jax.random.split(key, 20)
    D = D_MODEL
    return {
        "x": _normal(ks[0], (BATCH, SEQ, D), 1.0),
        "mla_w_in": _normal(ks[1], (N_MLA, D, MLA_IN), D ** -0.5),
        "mla_q_norm": 1.0 + _normal(ks[2], (N_MLA, MLA_Q_RANK), 0.02),
        "mla_kv_norm": 1.0 + _normal(ks[3], (N_MLA, MLA_KV_RANK), 0.02),
        "mla_w_uq": _normal(ks[4], (N_MLA, MLA_Q_RANK, MLA_HEADS, MLA_NOPE + MLA_ROPE), MLA_Q_RANK ** -0.5),
        "mla_w_ukv": _normal(ks[5], (N_MLA, MLA_KV_RANK, MLA_HEADS, MLA_NOPE + MLA_V), MLA_KV_RANK ** -0.5),
        "mla_w_o": _normal(ks[6], (N_MLA, MLA_HEADS * MLA_V, D), DN_BETA * (MLA_HEADS * MLA_V) ** -0.5),
        "dsa_w_in": _normal(ks[7], (N_DSA, D, DSA_IN), D ** -0.5),
        "dsa_w_o": _normal(ks[8], (N_DSA, DSA_HD, D), DN_BETA * DSA_HD ** -0.5),
        "peer_w_q": _normal(ks[9], (DEPTH, D, PEER_HEADS * PEER_QDIM), D ** -0.5),
        "peer_sub_keys": _normal(ks[10], (DEPTH, 2, PEER_HEADS, PEER_NKEYS, PEER_QDIM // 2), (PEER_QDIM // 2) ** -0.5),
        "peer_w_down": _normal(ks[11], (DEPTH, PEER_EXPERTS, D), D ** -0.5),
        "peer_w_up": _normal(ks[12], (DEPTH, PEER_EXPERTS, D), DN_BETA * PEER_HEADS ** -0.5),
        "ln_gain": 1.0 + _normal(ks[13], (DEPTH, 2, D), 0.02),
        "ln_bias": _normal(ks[14], (DEPTH, 2, D), 0.02),
    }

def second_block(x, mla_w_in, mla_q_norm, mla_kv_norm, mla_w_uq, mla_w_ukv, mla_w_o,
              dsa_w_in, dsa_w_o, peer_w_q, peer_sub_keys, peer_w_down, peer_w_up,
              ln_gain, ln_bias):
    for i in range(DEPTH):
        j = i // N_MIXERS
        if i % N_MIXERS == 0:
            m = _mla_mixer(x, mla_w_in[j], mla_q_norm[j], mla_kv_norm[j],
                           mla_w_uq[j], mla_w_ukv[j], mla_w_o[j])
        else:
            m = _dsa_mixer(x, dsa_w_in[j], dsa_w_o[j])
        x = _layernorm(DN_ALPHA * x + m, ln_gain[i, 0], ln_bias[i, 0])
        f = _peer(x, peer_w_q[i], peer_sub_keys[i], peer_w_down[i], peer_w_up[i])
        x = _layernorm(DN_ALPHA * x + f, ln_gain[i, 1], ln_bias[i, 1])
    return x


def setup_inputs(seed=0):
    out = dict(first_inputs(seed))
    for name, value in second_inputs(seed + 1).items():
        if name != "x":
            out[name + "_2"] = value
    return out


def reference(
    x, p, norm_ffn1, w_ffn1_gu, w_ffn1_down, norm_mix, w_qkv, q_norm, k_norm, w_o, w_pool_in,
    w_pool_grp, pool_scale, norm_ffn2, w_ffn2_gu, w_ffn2_down, norm_ple, w_ple_gate, w_ple_proj,
    mla_w_in_2, mla_q_norm_2, mla_kv_norm_2, mla_w_uq_2, mla_w_ukv_2, mla_w_o_2, dsa_w_in_2,
    dsa_w_o_2, peer_w_q_2, peer_sub_keys_2, peer_w_down_2, peer_w_up_2, ln_gain_2, ln_bias_2,
):
    x = first_block(
        x, p, norm_ffn1, w_ffn1_gu, w_ffn1_down, norm_mix, w_qkv, q_norm, k_norm, w_o,
        w_pool_in, w_pool_grp, pool_scale, norm_ffn2, w_ffn2_gu, w_ffn2_down, norm_ple,
        w_ple_gate, w_ple_proj,
    )
    return second_block(
        x, mla_w_in_2, mla_q_norm_2, mla_kv_norm_2, mla_w_uq_2, mla_w_ukv_2, mla_w_o_2,
        dsa_w_in_2, dsa_w_o_2, peer_w_q_2, peer_sub_keys_2, peer_w_down_2, peer_w_up_2,
        ln_gain_2, ln_bias_2,
    )


_drawn_inputs = setup_inputs


def setup_inputs(seed=0):
    import zlib

    import numpy as np

    out = dict(_drawn_inputs(seed))
    spreads = {}
    factors = {'q_norm': 3.008,
     'k_norm': 3.19,
     'norm_ple': 3.528,
     'mla_q_norm_2': 8.0,
     'mla_kv_norm_2': 8.0}
    for name, (base, spread) in spreads.items():
        noise = np.random.default_rng([zlib.crc32(name.encode()), seed]).standard_normal(out[name].shape)
        drawn = base * np.exp(spread * noise) if base else spread * noise
        out[name] = __import__('jax').numpy.asarray(drawn.astype(out[name].dtype))
    for name, factor in factors.items():
        out[name] = (out[name] * factor).astype(out[name].dtype)
    return out
```

```python
import numpy as np
from contextlib import ExitStack, contextmanager

import concourse.bass as bass
from concourse import mybir

F32 = mybir.dt.float32
F32R = mybir.dt.float32r
U32 = mybir.dt.uint32
ALU = mybir.AluOpType
ACT = mybir.ActivationFunctionType
AX_X = mybir.AxisListType.X

P = 128
D = 1024
T = 256
TB = T // P
KD = D // P
DEPTH = 2
D_FF = 2816
FC = D_FF // P
HEADS, HD = 16, 64
WINDOWS = (2, 4, 8, 16)
EPS, LN_EPS = 1e-6, 1e-5
ALPHA = (2 * DEPTH) ** 0.25
Q_RANK, KV_RANK, ROPE = 384, 256, 64
H2 = 8
IDX = 64
TOPK = min(256, T // 4)
NK = 128
K16 = 16
UNIT = 1024
RAW, SPLIT = 2, 4
PAIR = 384
NEG = -1e30
TAKEN = -3e38
TURN = 8

IDENT, IOTA, HALF, ONE, QG, KG, G_MLA = 0, 128, 256, 257, 258, 259, 260
G_NORM = 265
N_CONST = G_NORM + 8 * KD

ARENA = NK * T
A_Q, A_K, A_V, A_QT, A_KT = 0, 2048, 4096, 6144, 8192
A_STAY, A_LOGW = 10240, 16384
A_TMP, A_SOFT, A_LN = 22528, 24064, 25600
A_STICKC = 27136
A_FFN = 24576
A_XN, A_SQ = 28672, 30720
A_POOLC, A_SCALE = 10240, 12288
M_C, M_QR, M_ROT, M_QRT, M_KRD, M_KRT, M_RA, M_RB, M_SM, M_PT, M_ROPE = (
    0, 2048, 3072, 10240, 11264, 11520, 12288, 13312, 16384, 19456, 27136)
S_I, S_IROT, S_IT, S_KID, S_KIT, S_RA, S_RB, S_SM, S_PT, S_QROT, S_KROT, S_IDX, S_ROPE, S_RELU, S_W, S_SEL = (
    12288, 13568, 10240, 11264, 11520, 14592, 16640, 18688, 21760, 24832, 18688, 26880, 27648, 30720,
    31488, 32256)
E_Q, E_SK, E_S = 0, 4096, 28672
X_P0, X_P1, X_CA, X_CB, X_I1, X_I2, X_G, X_EQ = 0, 256, 512, 768, 1024, 1280, 1536, 1792
STICK_COLS, ROPE_COLS = PAIR + 2 * P, 768


def unit_plan():
    ffn = 3 * FC
    plan = []
    for i in range(DEPTH):
        plan += [("ffn", ffn)]
        plan += [("qkv", 3 * KD), ("wo", KD)] if i == 0 else [("pool", KD), ("grp", 2)]
        plan += [("ffn", ffn), ("gate", KD), ("ple", 3)]
    plan += [("mla_in", KD), ("mla_qr", 2), ("mla_qn", 3), ("mla_kn", 2), ("mla_v", 2), ("mla_o", KD)]
    plan += [("peer_q", 16), ("down", NK), ("up", NK)]
    plan += [("dsa_in", 4 * KD), ("dsa_o", KD)]
    plan += [("peer_q", 16), ("down", NK), ("up", NK)]
    return plan


TOPK_STEPS = 17
KEPT_MLA = 3 + 1 + DEPTH + 1
N_UNITS = sum(n for _, n in unit_plan()) + SPLIT
N_UNITS += N_UNITS % RAW


class Tally:

    def __init__(self, eng, start=()):
        self.eng, self.at, self.step, self.i = eng, dict(start), {}, None

    def value(self, sem):
        v = self.at.get(sem.name, 0)
        return v if self.i is None else v + self.step.get(sem.name, 0) * self.i

    def after(self, sem, n=1):
        self.at[sem.name] = self.at.get(sem.name, 0) + n
        return self.value(sem)

    skip = after

    @contextmanager
    def loop(self, turns, steps):
        base = dict(self.at)
        self.step = {s.name: n for s, n in steps}
        with self.eng.Fori(0, turns) as i:
            self.i = i
            yield i
        for name in set(self.at) | set(self.step):
            grew = self.at.get(name, 0) - base.get(name, 0)
            assert grew == self.step.get(name, 0), (name, grew, self.step.get(name, 0))
            self.at[name] = base.get(name, 0) + grew * turns
        self.i, self.step = None, {}


def program(nc, stream, x_in_dram, consts, stickc, poolc, scalec, ropec, lnc, subkeys, out):
    with ExitStack() as ctx:
        base = -(-nc.sbuf_base // 32) * 32
        arena = ctx.enter_context(nc.sbuf_tensor("arena", [P, ARENA], F32))
        h_hi = nc.alloc_sbuf_tensor_at("h_hi", [P, 2, T], F32R, offset=base + 4 * (A_FFN + 4 * T))
        h_lo = nc.alloc_sbuf_tensor_at("h_lo", [P, 2, T], F32R, offset=base + 4 * (A_FFN + 6 * T))

        def sb(name, shape, dt=F32):
            return ctx.enter_context(nc.sbuf_tensor(name, shape, dt))

        def sem(name):
            return ctx.enter_context(nc.semaphore(name))

        x = sb("x", [P, TB, D])
        act_hi = sb("act_hi", [P, KD, T], F32R)
        act_lo = sb("act_lo", [P, KD, T], F32R)
        raw = sb("raw", [P, RAW, UNIT])
        w_hi = sb("w_hi", [P, SPLIT, UNIT], F32R)
        w_lo = sb("w_lo", [P, SPLIT, UNIT], F32R)
        cst = sb("cst", [P, N_CONST])
        zero = sb("zero", [1, P], F32R)
        small = sb("small", [P, 96])
        stats = sb("stats", [P, 48])
        pad = sb("pad", [P, 2048])
        hot = sb("hot", [P, 3, T])
        rank = sb("rank", [P, 112])
        rank_u = sb("rank_u", [P, 80], U32)
        ps = ctx.enter_context(nc.psum_tensor("ps", [P, 8, 512], F32))

        landed = [sem(f"landed{s}") for s in range(RAW)]
        hi_done = sem("hi_done")
        lo_done = sem("lo_done")
        unit_used = sem("unit_used")
        x_in, consts_in, stick_in, pool_in, rope_in, ln_in, subkeys_in = (
            sem(n) for n in ("x_in", "consts_in", "stick_in", "pool_in", "rope_in", "ln_in", "subkeys_in"))
        act_step = sem("act_step")
        dve_step = sem("dve_step")
        pool_step = sem("pool_step")
        pool_past = sem("pool_past")
        x_ready = sem("x_ready")
        stat_ready = sem("stat_ready")
        mean_ready = sem("mean_ready")
        var_ready = sem("var_ready")
        rstd_ready = sem("rstd_ready")
        rows_ready = sem("rows_ready")
        turned = sem("turned")
        turned_hi = sem("turned_hi")
        act_ready = sem("act_ready")
        turned_kept = sem("turned_kept")
        acc_kept = sem("acc_kept")
        silu_done = sem("silu_done")
        h_ready = sem("h_ready")
        h_hi_ready = sem("h_hi_ready")
        h_lo_ready = sem("h_lo_ready")
        z_done = sem("z_done")
        ln_done = sem("ln_done")
        soft_done = sem("soft_done")
        z_used = sem("z_used")
        stay_ready = sem("stay_ready")
        c_done = sem("c_done")
        c_used = sem("c_used")
        w_exp = sem("w_exp")
        w_ready = sem("w_ready")
        o_done = sem("o_done")
        o_hi = sem("o_hi")
        i_done = sem("i_done")
        relu_done = sem("relu_done")
        relu_used = sem("relu_used")
        s_done = sem("s_done")
        s_used = sem("s_used")
        max_ready = sem("max_ready")
        e_done = sem("e_done")
        p_ready = sem("p_ready")
        p_turned = sem("p_turned")
        p_kept = sem("p_kept")
        scores_done = sem("scores_done")
        work_kept = sem("work_kept")
        scores_taken = sem("scores_taken")
        best_ready = sem("best_ready")
        gates_exp = sem("gates_exp")
        ranks_ready = sem("ranks_ready")
        hot_ready = sem("hot_ready")
        hot1_done = sem("hot1_done")
        hot2_done = sem("hot2_done")
        gates_done = sem("gates_done")
        gates_used = sem("gates_used")
        eh_hi = sem("eh_hi")
        eh_ready = sem("eh_ready")
        out_done = sem("out_done")

        ident = cst[:, IDENT:IDENT + P]
        iota = cst[:, IOTA:IOTA + P]

        def area(at, n):
            return arena[:, at:at + n]

        def tok(at, n):
            return area(at, TB * n).rearrange("p (b n) -> p b n", b=TB)

        def blk(at, n, w=T):
            return area(at, n * w).rearrange("p (k t) -> p k t", k=n)

        def acc(s, n=D):
            return ps[:, 4 * s:4 * s + 4, :].rearrange("p (b h) c -> p b (h c)", b=TB)[:, :, 0:n]

        xn, sq = tok(A_XN, D), tok(A_SQ, 1024)
        q_tok, k_tok, v_tok = tok(A_Q, D), tok(A_K, D), tok(A_V, D)
        qT, kT = blk(A_QT, KD), blk(A_KT, KD)
        silu, prod = blk(A_FFN, 2), blk(A_FFN + 2 * T, 2)
        keep = arena[:, :].rearrange("p (c t) -> p c t", t=T)
        stay, logw = blk(A_STAY, HEADS, PAIR), blk(A_LOGW, HEADS, PAIR)
        sigma = tok(A_Q, D)
        ln_g, ln_b = pad[:, 0:D], pad[:, D:2 * D]
        N_PAIRS = HEADS // 2
        LAST = DEPTH - 1
        block = ctx.enter_context(nc.Block())

        @block.sync
        def _(sp):
            for u in range(RAW):
                sp.dma_start(raw[:, u, :], stream[u]).then_inc(landed[u], 16)
            with sp.Fori(1, N_UNITS // RAW) as i:
                for s in range(RAW):
                    sp.wait_ge(lo_done, i * RAW + (s - RAW + 1))
                    sp.dma_start(raw[:, s, :], stream[i * RAW + s]).then_inc(landed[s], 16)
            sp.wait_ge(x_ready, TB * (4 * DEPTH + 2 * DEPTH))
            sp.dma_start(out.rearrange("(b p) d -> p b d", b=TB), x[:, :, :]).then_inc(out_done, 16)
            sp.wait_ge(out_done, 16)

        @block.gpsimd
        def _(pool):
            t = Tally(pool)
            pool.dma_start(x[:, :, :], x_in_dram.rearrange("(b p) d -> p b d", b=TB)).then_inc(x_in, 16)
            pool.dma_start(cst[:, :], consts).then_inc(consts_in, 16)
            pool.wait_ge(consts_in, 16)

            def power(src, dst, n):
                pool.wait_ge(var_ready, t.after(var_ready))
                pool.tensor_tensor(small[:, dst:dst + n], small[:, src:src + n],
                                   cst[:, HALF:HALF + 1].broadcast_to([P, n]), ALU.pow).then_inc(rstd_ready, 1)

            def x_changed():
                pool.wait_ge(x_ready, t.after(x_ready, TB))

            def stick_breaking():
                m = area(A_STICKC, PAIR).unsqueeze(1).broadcast_to([P, 2, PAIR])
                soft = blk(A_SOFT, 4, PAIR)
                for p in range(N_PAIRS):
                    pool.wait_ge(soft_done, t.after(soft_done))
                    pool.tensor_tensor(stay[:, 2 * p:2 * p + 2, :], soft[:, 2 * (p % 2):2 * (p % 2) + 2, :], m,
                                       ALU.mult).then_inc(stay_ready, 1)
                for p in range(N_PAIRS):
                    pool.wait_ge(w_exp, t.after(w_exp))
                    w = logw[:, 2 * p:2 * p + 2, :]
                    pool.tensor_tensor(w, w, m, ALU.mult).then_inc(w_ready, 1)

            for i in range(DEPTH):
                power(0, 16, TB)
                x_changed()
                if i == 0:
                    pool.dma_start(area(A_STICKC, STICK_COLS), stickc).then_inc(stick_in, 16)
                else:
                    pool.dma_start(area(A_POOLC, 2048), poolc).then_inc(pool_in, 16)
                    pool.dma_start(area(A_SCALE, D), scalec).then_inc(pool_in, 16)
                power(0, 16, TB)
                if i == 0:
                    power(32, 64, 32)
                    power(32, 64, 32)
                    pool.wait_ge(stick_in, t.after(stick_in, 16))
                    stick_breaking()
                x_changed()
                power(0, 16, TB)
                x_changed()
                power(0, 16, TB)
                x_changed()
            for i in range(DEPTH):
                at = M_ROPE if i == 0 else S_ROPE
                pool.dma_start(area(at, ROPE_COLS), ropec).then_inc(rope_in, 16)
                pool.dma_start(pad[:, :], lnc[2 * i]).then_inc(ln_in, 16)
                if i == 0:
                    power(0, 16, 4)
                power(0, 16, TB)
                x_changed()
                pool.dma_start(area(E_SK, 2048), subkeys[i]).then_inc(subkeys_in, 16)
                pool.wait_ge(hot_ready, t.after(hot_ready, 2))

                def one_hots(q, s):
                    first = small[:, 80 + 4 * s:84 + 4 * s]
                    pool.tensor_copy(first, hot[:, 0, bass.ds(q * 4, 4)]).then_inc(pool_step, 1)
                    pool.wait_ge(pool_step, t.after(pool_step))
                    pool.sem_inc(pool_past, 1)
                    for j in range(4):
                        ins = pool.tensor_scalar(pad[:, 1024 * s + NK * j:1024 * s + NK * (j + 1)], iota,
                                                 first[:, j:j + 1], None, ALU.is_equal)
                    ins.then_inc(hot1_done, 1)

                for s in range(2):
                    one_hots(s, s)
                with t.loop(T // 8 - 1, [(gates_done, 2), (pool_step, 2)]) as n:
                    for s in range(2):
                        pool.wait_ge(gates_done, t.after(gates_done))
                        one_hots(n * 2 + (2 + s), s)
                t.skip(gates_done, 2)
                pool.wait_ge(gates_used, t.after(gates_used, T // 4))
                pool.dma_start(pad[:, :], lnc[2 * i + 1]).then_inc(ln_in, 16)
                power(0, 16, TB)
                x_changed()

        @block.scalar
        def _(act):
            t = Tally(act, {unit_used.name: -SPLIT})
            units = [0]
            xs = [0]

            def step(ins):
                ins.then_inc(act_step, 1)
                act.wait_ge(act_step, t.after(act_step))

            def x_changed():
                if xs[0]:
                    act.wait_ge(x_ready, t.after(x_ready, TB))
                else:
                    act.wait_ge(x_in, 16)
                xs[0] += 1

            def split(n=1):
                for _ in range(n):
                    u = units[0]
                    units[0] += 1
                    act.wait_ge(landed[u % RAW], t.after(landed[u % RAW], 16))
                    free = t.after(unit_used)
                    if u >= SPLIT:
                        act.wait_ge(unit_used, free)
                    act.activation(w_hi[:, u % SPLIT, :], raw[:, u % RAW, :], ACT.Copy).then_inc(hi_done, 1)

            def unit_steps(n):
                return [(landed[s], 16 * n // RAW) for s in range(RAW)] + [(unit_used, n)]

            def looped_split(turns, n):
                with t.loop(turns, unit_steps(n)):
                    split(n)

            def squares():
                x_changed()
                for b in range(TB):
                    act.activation(sq[:, b, :], x[:, b, :], ACT.Square,
                                   accum_out=small[:, 8 + b:9 + b]).then_inc(stat_ready, 1)

            def turned_high(gain=None, banks=4):
                for b in range(banks):
                    act.wait_ge(turned, t.after(turned))
                    if gain is None:
                        ins = act.activation(act_hi[:, 2 * b:2 * b + 2, :], ps[:, 4 + b, :], ACT.Copy)
                    else:
                        for k in (2 * b, 2 * b + 1):
                            ins = act.activation(act_hi[:, k, :], ps[:, 4 + b, (k % 2) * T:(k % 2) * T + T],
                                                 ACT.Copy, scale=cst[:, gain + k:gain + k + 1])
                    ins.then_inc(turned_hi, 1)

            def keep_turned(dst, banks, gain=1.0):
                for n, b in enumerate(banks):
                    act.wait_ge(turned, t.after(turned))
                    act.activation(dst[:, 512 * n:512 * n + 512], ps[:, b, :], ACT.Copy,
                                   scale=gain).then_inc(turned_kept, 1)

            def product_done():
                act.wait_ge(unit_used, t.value(unit_used))

            def keep_acc(dst, s, n=D, func=ACT.Copy):
                product_done()
                for b in range(TB):
                    ins = act.activation(dst[:, b, :], acc(s, n)[:, b, :], func)
                ins.then_inc(acc_kept, 1)

            def norm(g):
                squares()
                turned_high(G_NORM + KD * g)

            def ffn():
                def chunk(s, units_after=1):
                    act.wait_ge(unit_used, t.value(unit_used) + units_after)
                    act.activation(silu[:, s, :], ps[:, 4 + s, 0:T], ACT.Silu).then_inc(silu_done, 1)
                    split()
                    act.wait_ge(h_ready, t.after(h_ready))
                    act.activation(h_hi[:, s, :], prod[:, s, :], ACT.Copy).then_inc(h_hi_ready, 1)
                    split(2)

                chunk(0, 2)
                with t.loop(5, [(h_ready, 4)] + unit_steps(12)):
                    for j in range(4):
                        chunk((j + 1) % 2)
                chunk(1)

            def stick_breaking():
                tmp, ln = blk(A_TMP, 4, PAIR), blk(A_LN, 4, PAIR)
                for p in range(N_PAIRS):
                    act.wait_ge(z_done, t.after(z_done))
                    z = ps[:, 2 * (p % 4):2 * (p % 4) + 2, 0:PAIR]
                    m = tmp[:, 2 * (p % 2):2 * (p % 2) + 2, :]
                    step(act.activation(m, z, ACT.Abs))
                    step(act.activation(m, m, ACT.Exp, scale=-1.0))
                    if p >= 2:
                        act.wait_ge(z_used, t.after(z_used))
                    act.activation(ln[:, 2 * (p % 2):2 * (p % 2) + 2, :], m, ACT.Ln,
                                   bias=cst[:, ONE:ONE + 1]).then_inc(ln_done, 1)
                t.skip(z_used, 2)
                for p in range(N_PAIRS + 1):
                    if p < N_PAIRS:
                        act.wait_ge(c_used, t.after(c_used))
                        w = logw[:, 2 * p:2 * p + 2, :]
                        act.activation(w, w, ACT.Exp).then_inc(w_exp, 1)
                    if p >= 1:
                        heads_high(p - 1, 4 + (p - 1) % 4)

            def heads_high(k, bank):
                act.wait_ge(o_done, t.after(o_done))
                act.activation(act_hi[:, k, :], ps[:, bank, 0:T], ACT.Copy).then_inc(o_hi, 1)

            def attention(sm_at, pt_at):
                sm, pT = blk(sm_at, H2, PAIR), blk(pt_at, H2, PAIR)
                for n in range(H2 + 2):
                    if n < H2:
                        act.wait_ge(max_ready, t.after(max_ready))
                        for b, (lo, hi) in enumerate(((0, P), (P, PAIR))):
                            ins = act.activation(sm[:, n, lo:hi], sm[:, n, lo:hi], ACT.Exp,
                                                 bias=stats[:, 2 * n + b:2 * n + b + 1],
                                                 accum_out=stats[:, 16 + 2 * n + b:17 + 2 * n + b])
                        ins.then_inc(e_done, 1)
                    if 1 <= n <= H2:
                        act.wait_ge(p_turned, t.after(p_turned))
                        act.activation(pT[:, n - 1, :], ps[:, 4 + (n - 1) % 2, 0:PAIR], ACT.Copy).then_inc(p_kept, 1)
                    if n >= 2:
                        heads_high(n - 2, 6 + n % 2)

            def layer_norm():
                for b in range(TB):
                    act.wait_ge(mean_ready, t.after(mean_ready))
                    act.activation(sq[:, b, :], x[:, b, :], ACT.Square,
                                   bias=small[:, 12 + b:13 + b],
                                   accum_out=small[:, 10 + b:11 + b]).then_inc(stat_ready, 1)

            split(SPLIT)
            act.wait_ge(consts_in, 16)
            for i in range(DEPTH):
                norm(4 * i)
                ffn()
                norm(4 * i + 1)
                if i == 0:
                    split(KD)
                    keep_acc(q_tok, 0)
                    split(KD)
                    keep_acc(k_tok, 1)
                    split(KD)
                    keep_acc(v_tok, 0)
                    keep_turned(area(A_QT, 2048), range(4, 8), cst[:, QG:QG + 1])
                    keep_turned(area(A_KT, 2048), range(4), cst[:, KG:KG + 1])
                    stick_breaking()
                    split(KD)
                else:
                    split(KD)
                    keep_acc(q_tok, 0)
                    turned_high()
                    split(2)
                norm(4 * i + 2)
                ffn()
                norm(4 * i + 3)
                split(KD)
                keep_acc(sigma, 0, D, ACT.Sigmoid)
                split(3)
            for i in range(DEPTH):
                x_changed()
                turned_high()
                if i == 0:
                    c_tok = tok(M_C, 704)
                    split(KD)
                    product_done()
                    for b in range(TB):
                        ins = act.activation(c_tok[:, b, :], acc(0, 704)[:, b, :], ACT.Copy)
                    ins.then_inc(acc_kept, 1)
                    act.wait_ge(acc_kept, KEPT_MLA)
                    for c, (lo, hi) in enumerate(((0, Q_RANK), (Q_RANK, Q_RANK + KV_RANK))):
                        for b in range(TB):
                            ins = act.activation(sq[:, b, lo:hi], c_tok[:, b, lo:hi], ACT.Square,
                                                 accum_out=small[:, 8 + 2 * c + b:9 + 2 * c + b])
                    ins.then_inc(stat_ready, 1)
                    for b in range(3):
                        act.wait_ge(turned, t.after(turned))
                        for k in range(2 * b, min(2 * b + 2, 5)):
                            ins = act.activation(act_hi[:, k, :], ps[:, 4 + b, (k % 2) * T:(k % 2) * T + T],
                                                 ACT.Copy, scale=cst[:, G_MLA + k:G_MLA + k + 1])
                        if b == 2:
                            ins = act.activation(area(M_KRT, T), ps[:, 6, T:2 * T], ACT.Copy)
                        ins.then_inc(turned_hi, 1)
                    split(2)
                    product_done()
                    for b in range(TB):
                        ins = act.activation(tok(M_QR, 512)[:, b, :], ps[:, b, :], ACT.Copy)
                    ins.then_inc(acc_kept, 1)
                    split(3)
                    product_done()
                    for b in range(4):
                        ins = act.activation(area(A_QT + 512 * b, 512), ps[:, 4 + b, :], ACT.Copy)
                    ins.then_inc(acc_kept, 1)
                    split(2)
                    product_done()
                    for b in range(4):
                        ins = act.activation(area(A_KT + 512 * b, 512), ps[:, b, :], ACT.Copy)
                    ins.then_inc(acc_kept, 1)
                    split(2)
                    keep_acc(v_tok, 1)
                    keep_turned(area(M_QRT, 1024), range(2))
                    attention(M_SM, M_PT)
                else:
                    split(KD)
                    keep_acc(tok(S_I, 584), 0, 584)
                    split(KD)
                    keep_acc(q_tok, 1)
                    split(KD)
                    keep_acc(k_tok, 0)
                    split(KD)
                    keep_acc(v_tok, 1)
                    keep_turned(area(S_IT, 1024), range(2))
                    act.wait_ge(turned, t.after(turned))
                    act.activation(area(S_KIT, T), ps[:, 2, 0:T], ACT.Copy).then_inc(turned_kept, 1)
                    keep_turned(area(A_QT, 2048), range(4, 8))
                    keep_turned(area(A_KT, 2048), range(4))
                    relu = blk(S_RELU, 2, PAIR)
                    for h in range(H2):
                        act.wait_ge(i_done, t.after(i_done))
                        if h >= 2:
                            act.wait_ge(relu_used, t.after(relu_used))
                        act.activation(relu[:, h % 2, :], ps[:, 4 + h % 4, 0:PAIR], ACT.Relu).then_inc(relu_done, 1)
                    t.skip(relu_used, 2)
                    attention(S_SM, S_PT)
                split(KD)
                layer_norm()

                x_changed()
                turned_high()
                with t.loop(4, unit_steps(4)) as n:
                    for j in range(4):
                        act.wait_ge(unit_used, t.value(unit_used) + 1)
                        act.activation(arena[:, bass.ds(n * 1024 + (E_Q + T * j), T)], ps[:, 4 + j, 0:T],
                                       ACT.Copy).then_inc(work_kept, 1)
                        split()
                for r in range(8):
                    act.wait_ge(scores_done, t.after(scores_done))
                    act.activation(area(E_S + 512 * r, 512), ps[:, 4 + r % 4, :], ACT.Copy).then_inc(work_kept, 1)
                with t.loop(NK // TURN, [(scores_taken, 1)] + unit_steps(TURN)) as n:
                    for j in range(TURN):
                        act.wait_ge(unit_used, t.value(unit_used) + 1)
                        if j == TURN - 1:
                            act.wait_ge(scores_taken, t.after(scores_taken))
                        act.activation(keep[:, bass.ds(n * TURN + j, 1), :].rearrange("p a t -> p (a t)"),
                                       ps[:, 4 + j % 4, 0:T], ACT.Gelu).then_inc(work_kept, 1)
                        split()
                act.wait_ge(best_ready, t.after(best_ready))
                act.activation(pad[:, X_G:X_G + T], pad[:, X_G:X_G + T], ACT.Exp).then_inc(gates_exp, 1)
                for b in range(2):
                    act.wait_ge(turned, t.after(turned))
                    act.activation(hot[:, 2 * b:min(2 * b + 2, 3), :].rearrange("p a t -> p (a t)"),
                                   ps[:, 4 + b, 0:(512 if b == 0 else T)], ACT.Copy).then_inc(hot_ready, 1)
                act.wait_ge(gates_used, t.after(gates_used, T // 4))

                def chunk_high(c, j):
                    act.activation(act_hi[:, j, :], keep[:, bass.ds(c, 1), :].rearrange("p a t -> p (a t)"),
                                   ACT.Copy).then_inc(eh_hi, 1)

                for j in range(KD):
                    chunk_high(j, j)
                with t.loop(NK // TURN - 1, unit_steps(TURN)) as n:
                    for j in range(TURN):
                        split()
                        chunk_high(n * TURN + (TURN + j), j)
                split(TURN)
                layer_norm()

        @block.vector
        def _(dve):
            t = Tally(dve)
            units = [0]

            def step(ins):
                ins.then_inc(dve_step, 1)
                dve.wait_ge(dve_step, t.after(dve_step))

            def split(n=1):
                for _ in range(n):
                    u = units[0]
                    units[0] += 1
                    dve.wait_ge(hi_done, t.after(hi_done))
                    dve.tensor_tensor(w_lo[:, u % SPLIT, :], raw[:, u % RAW, :],
                                      w_hi[:, u % SPLIT, :].bitcast(F32), ALU.subtract).then_inc(lo_done, 1)

            def product_done():
                dve.wait_ge(unit_used, t.at[hi_done.name] - SPLIT)

            def variance(n=TB, at=8):
                dve.wait_ge(stat_ready, t.after(stat_ready, n))
                dve.tensor_scalar(small[:, 0:TB], small[:, at:at + TB], 1.0 / D,
                                  EPS if at == 8 else LN_EPS, ALU.mult, ALU.add).then_inc(var_ready, 1)
                dve.wait_ge(rstd_ready, t.after(rstd_ready))

            def turned_low(gain=None):
                for b in range(4):
                    dve.wait_ge(turned_hi, t.after(turned_hi))
                    if gain is None:
                        ins = dve.tensor_tensor(act_lo[:, 2 * b:2 * b + 2, :].rearrange("p k t -> p (k t)"),
                                                ps[:, 4 + b, :],
                                                act_hi[:, 2 * b:2 * b + 2, :].rearrange("p k t -> p (k t)").bitcast(F32),
                                                ALU.subtract)
                    else:
                        for k in (2 * b, 2 * b + 1):
                            ins = low_with_gain(k, ps[:, 4 + b, (k % 2) * T:(k % 2) * T + T], gain)
                    ins.then_inc(act_ready, 1)

            def low_with_gain(k, src, gain):
                return dve.scalar_tensor_tensor(act_lo[:, k, :], src, cst[:, gain + k:gain + k + 1],
                                                act_hi[:, k, :].bitcast(F32), ALU.mult, ALU.subtract)

            def norm(g):
                variance()
                for b in range(TB):
                    dve.tensor_scalar(xn[:, b, :], x[:, b, :], small[:, 16 + b:17 + b], None,
                                      ALU.mult).then_inc(rows_ready, 1)
                turned_low(G_NORM + KD * g)

            def ffn():
                def chunk(s):
                    dve.wait_ge(silu_done, t.after(silu_done))
                    dve.tensor_tensor(prod[:, s, :], silu[:, s, :], ps[:, 4 + s, T:2 * T],
                                      ALU.mult).then_inc(h_ready, 1)
                    split()
                    dve.wait_ge(h_hi_ready, t.after(h_hi_ready))
                    dve.tensor_tensor(h_lo[:, s, :], prod[:, s, :], h_hi[:, s, :].bitcast(F32),
                                      ALU.subtract).then_inc(h_lo_ready, 1)
                    split(2)

                chunk(0)
                with t.loop(5, [(silu_done, 4), (h_hi_ready, 4), (hi_done, 12)]):
                    for j in range(4):
                        chunk((j + 1) % 2)
                chunk(1)
                product_done()
                for b in range(TB):
                    dve.scalar_tensor_tensor(x[:, b, :], acc(0)[:, b, :], 0.5, x[:, b, :], ALU.mult,
                                             ALU.add).then_inc(x_ready, 1)

            def head_norm(rows, scale, eps):
                dve.wait_ge(acc_kept, t.after(acc_kept))
                flat = rows.rearrange("p b n -> p (b n)")
                sqf = sq.rearrange("p b n -> p (b n)")
                step(dve.tensor_tensor(sqf, flat, flat, ALU.mult))
                step(dve.tensor_reduce(small[:, 32:64], sqf.rearrange("p (h d) -> p h d", d=HD), AX_X, ALU.add))
                dve.tensor_scalar(small[:, 32:64], small[:, 32:64], scale, eps, ALU.mult,
                                  ALU.add).then_inc(var_ready, 1)
                dve.wait_ge(rstd_ready, t.after(rstd_ready))
                heads = flat.rearrange("p (h d) -> p h d", d=HD)
                dve.tensor_tensor(heads, heads, small[:, 64:96].unsqueeze(2).broadcast_to([P, 32, HD]),
                                  ALU.mult).then_inc(rows_ready, 1)

            def heads_low(k, bank):
                dve.wait_ge(o_hi, t.after(o_hi))
                dve.tensor_tensor(act_lo[:, k, :], ps[:, bank, 0:T], act_hi[:, k, :].bitcast(F32),
                                  ALU.subtract).then_inc(act_ready, 1)

            def stick_breaking():
                ln, soft = blk(A_LN, 4, PAIR), blk(A_SOFT, 4, PAIR)
                for p in range(N_PAIRS):
                    s = slice(2 * (p % 2), 2 * (p % 2) + 2)
                    z = ps[:, 2 * (p % 4):2 * (p % 4) + 2, 0:PAIR]
                    dve.wait_ge(ln_done, t.after(ln_done))
                    if p >= 2:
                        dve.wait_ge(stay_ready, t.after(stay_ready))
                    dve.scalar_tensor_tensor(soft[:, s, :], z, 0.0, ln[:, s, :], ALU.max,
                                             ALU.add).then_inc(soft_done, 1)
                    dve.scalar_tensor_tensor(logw[:, 2 * p:2 * p + 2, :], z, 0.0, ln[:, s, :], ALU.min,
                                             ALU.subtract).then_inc(z_used, 1)
                t.skip(stay_ready, 2)
                dve.wait_ge(z_used, N_PAIRS)
                for p in range(N_PAIRS + 2):
                    if p < N_PAIRS:
                        dve.wait_ge(c_done, t.after(c_done))
                        w = logw[:, 2 * p:2 * p + 2, :]
                        dve.tensor_tensor(w, w, ps[:, 2 * (p % 2):2 * (p % 2) + 2, 0:PAIR],
                                          ALU.subtract).then_inc(c_used, 1)
                    if p >= 2:
                        heads_low(p - 2, 4 + (p - 2) % 4)

            def rope(dst, src, ra, rb, at, half):
                n, h = src.shape[1], src.shape[2]
                cos, sin = (area(a, TB * half).rearrange("p (b d) -> p b d", b=TB).unsqueeze(2)
                            .broadcast_to([P, TB, h, half]) for a in at)
                x1, x2 = src[:, :, :, 0:half], src[:, :, :, half:2 * half]
                a1, a2 = ra[:, :, :, 0:half], ra[:, :, :, half:2 * half]
                b1, b2 = rb[:, :, :, 0:half], rb[:, :, :, half:2 * half]
                dve.tensor_tensor(a1, x1, cos, ALU.mult)
                dve.tensor_tensor(b1, x2, sin, ALU.mult)
                dve.tensor_tensor(a2, x2, cos, ALU.mult)
                step(dve.tensor_tensor(b2, x1, sin, ALU.mult))
                dve.tensor_tensor(dst[:, :, :, 0:half], a1, b1, ALU.subtract)
                return dve.tensor_tensor(dst[:, :, :, half:2 * half], a2, b2, ALU.add)

            def heads_of(at, h, d, row=None, off=0):
                row = row or h * d
                return tok(at, row)[:, :, off:off + h * d].rearrange("p b (h d) -> p b h d", h=h)

            def attention(sm_at, mask, scale):
                sm = blk(sm_at, H2, PAIR)
                parts = ((0, P), (P, PAIR))
                for n in range(H2 + 3):
                    if n < H2:
                        dve.wait_ge(s_done, t.after(s_done))
                        ins = dve.scalar_tensor_tensor(sm[:, n, :], ps[:, n % 4, 0:PAIR], scale, mask,
                                                       ALU.mult, ALU.add)
                        ins.then_inc(s_used, 1)
                        dve.wait_ge(s_used, t.after(s_used))
                        for b, (lo, hi) in enumerate(parts):
                            ins = dve.tensor_reduce(stats[:, 2 * n + b:2 * n + b + 1], sm[:, n, lo:hi], AX_X,
                                                    ALU.max, negate=True)
                        ins.then_inc(max_ready, 1)
                    if 1 <= n <= H2:
                        m = n - 1
                        dve.wait_ge(e_done, t.after(e_done))
                        step(dve.reciprocal(stats[:, 32 + 2 * (m % 8):34 + 2 * (m % 8)], stats[:, 16 + 2 * m:18 + 2 * m]))
                        for b, (lo, hi) in enumerate(parts):
                            ins = dve.tensor_scalar(sm[:, m, lo:hi], sm[:, m, lo:hi],
                                                    stats[:, 32 + 2 * m + b:33 + 2 * m + b], None, ALU.mult)
                        ins.then_inc(p_ready, 1)
                    if n >= 3:
                        heads_low(n - 3, 6 + (n - 3) % 2)

            def layer_norm():
                product_done()
                for b in range(TB):
                    step(dve.scalar_tensor_tensor(x[:, b, :], x[:, b, :], ALPHA, acc(0)[:, b, :], ALU.mult,
                                                  ALU.add, accum_out=small[:, 8 + b:9 + b]))
                    dve.tensor_scalar(small[:, 12 + b:13 + b], small[:, 8 + b:9 + b], -1.0 / D, None,
                                      ALU.mult).then_inc(mean_ready, 1)
                variance(TB, 10)
                dve.wait_ge(mean_ready, t.after(mean_ready, TB))
                dve.wait_ge(ln_in, t.after(ln_in, 16))
                for b in range(TB):
                    xb = x[:, b, :]
                    step(dve.tensor_scalar(xb, xb, small[:, 12 + b:13 + b], small[:, 16 + b:17 + b], ALU.add,
                                           ALU.mult))
                    step(dve.tensor_tensor(xb, xb, ln_g, ALU.mult))
                    dve.tensor_tensor(xb, xb, ln_b, ALU.add).then_inc(x_ready, 1)

            step(dve.memset(zero[:, :].bitcast(F32), 0.0))
            split(SPLIT)
            dve.wait_ge(x_in, 16)
            dve.wait_ge(consts_in, 16)
            for i in range(DEPTH):
                norm(4 * i)
                ffn()
                norm(4 * i + 1)
                if i == 0:
                    split(KD)
                    head_norm(q_tok, 1.0, HD * EPS)
                    split(KD)
                    head_norm(k_tok, 1.0 / HD, EPS)
                    split(KD)
                    t.skip(acc_kept)
                    stick_breaking()
                    split(KD)
                    product_done()
                    for b in range(TB):
                        dve.tensor_tensor(x[:, b, :], acc(0)[:, b, :], x[:, b, :], ALU.add).then_inc(x_ready, 1)
                else:
                    split(KD)
                    t.skip(acc_kept)
                    turned_low()
                    split(2)
                    dve.wait_ge(pool_in, t.after(pool_in, 32))
                    product_done()
                    for b in range(TB):
                        step(dve.tensor_tensor(sq[:, b, :], acc(0)[:, b, :], area(A_SCALE, D), ALU.mult))
                        dve.tensor_tensor(x[:, b, :], sq[:, b, :], x[:, b, :], ALU.add).then_inc(x_ready, 1)
                norm(4 * i + 2)
                ffn()
                norm(4 * i + 3)
                split(KD)
                split(3)
                dve.wait_ge(acc_kept, t.after(acc_kept))
                product_done()
                for b in range(TB):
                    step(dve.tensor_tensor(sq[:, b, :], acc(1)[:, b, :], sigma[:, b, :], ALU.mult))
                    dve.tensor_tensor(x[:, b, :], sq[:, b, :], x[:, b, :], ALU.add).then_inc(x_ready, 1)
            for i in range(DEPTH):
                turned_low()
                if i == 0:
                    c_tok = tok(M_C, 704)
                    split(KD)
                    dve.wait_ge(acc_kept, t.after(acc_kept))
                    dve.wait_ge(rope_in, t.after(rope_in, 16))
                    tables = (M_ROPE, M_ROPE + 64)
                    krd = tok(M_KRD, P)
                    kr4 = lambda off: krd[:, :, off:off + ROPE].unsqueeze(2)
                    step(rope(kr4(0), heads_of(M_C, 1, ROPE, 704, 640), heads_of(M_RA, 1, ROPE),
                              heads_of(M_RB, 1, ROPE), tables, 32))
                    dve.tensor_copy(krd[:, :, ROPE:P], krd[:, :, 0:ROPE])
                    dve.wait_ge(stat_ready, t.after(stat_ready))
                    dve.tensor_scalar(small[:, 0:2], small[:, 8:10], 1.0 / Q_RANK, EPS, ALU.mult, ALU.add)
                    dve.tensor_scalar(small[:, 2:4], small[:, 10:12], 1.0 / KV_RANK, EPS, ALU.mult,
                                      ALU.add).then_inc(var_ready, 1)
                    dve.wait_ge(rstd_ready, t.after(rstd_ready))
                    for c, (lo, hi) in enumerate(((0, Q_RANK), (Q_RANK, Q_RANK + KV_RANK))):
                        for b in range(TB):
                            ins = dve.tensor_scalar(c_tok[:, b, lo:hi], c_tok[:, b, lo:hi],
                                                    small[:, 16 + 2 * c + b:17 + 2 * c + b], None, ALU.mult)
                    ins.then_inc(rows_ready, 1)
                    for b in range(3):
                        dve.wait_ge(turned_hi, t.after(turned_hi))
                        for k in range(2 * b, min(2 * b + 2, 5)):
                            ins = low_with_gain(k, ps[:, 4 + b, (k % 2) * T:(k % 2) * T + T], G_MLA)
                        ins.then_inc(act_ready, 1)
                    split(2)
                    dve.wait_ge(acc_kept, t.after(acc_kept))
                    rope(heads_of(M_ROT, H2, ROPE), heads_of(M_QR, H2, ROPE), heads_of(M_RA, H2, ROPE),
                         heads_of(M_RB, H2, ROPE), tables, 32).then_inc(rows_ready, 1)
                    split(3)
                    split(2)
                    split(2)
                    t.skip(acc_kept, 3)
                    attention(M_SM, area(M_ROPE + 128, PAIR), (P + ROPE) ** -0.5)
                else:
                    split(KD)
                    dve.wait_ge(acc_kept, t.after(acc_kept))
                    dve.wait_ge(rope_in, t.after(rope_in, 16))
                    tables = (S_ROPE, S_ROPE + 64)
                    wide = (S_ROPE + 512, S_ROPE + 640)
                    i_tok = tok(S_I, 584)
                    kid = tok(S_KID, P)
                    rope(heads_of(S_IROT, H2, IDX), heads_of(S_I, H2, IDX, 584), heads_of(S_RA, H2, IDX),
                         heads_of(S_RB, H2, IDX), tables, 32)
                    step(rope(kid[:, :, 0:IDX].unsqueeze(2), heads_of(S_I, 1, IDX, 584, 512),
                              heads_of(S_RA + 1024, 1, IDX), heads_of(S_RB + 1024, 1, IDX), tables, 32))
                    dve.tensor_scalar(i_tok[:, :, 576:584], i_tok[:, :, 576:584], (H2 * IDX) ** -0.5, None, ALU.mult)
                    dve.tensor_copy(kid[:, :, IDX:P], kid[:, :, 0:IDX]).then_inc(rows_ready, 1)
                    split(KD)
                    dve.wait_ge(acc_kept, t.after(acc_kept))
                    rope(heads_of(S_QROT, H2, P), heads_of(A_Q, H2, P), heads_of(S_RA, H2, P),
                         heads_of(S_RB, H2, P), wide, 64).then_inc(rows_ready, 1)
                    split(KD)
                    dve.wait_ge(acc_kept, t.after(acc_kept))
                    rope(heads_of(S_KROT, H2, P), heads_of(A_K, H2, P), heads_of(S_RA, H2, P),
                         heads_of(S_RB, H2, P), wide, 64).then_inc(rows_ready, 1)
                    split(KD)
                    t.skip(acc_kept)
                    relu, score = blk(S_RELU, 2, PAIR), area(S_IDX, PAIR)
                    for h in range(H2):
                        dve.wait_ge(relu_done, t.after(relu_done))
                        for b, (lo, hi) in enumerate(((0, P), (P, PAIR))):
                            w = i_tok[:, b, 576 + h:577 + h]
                            r = relu[:, h % 2, lo:hi]
                            if h == 0:
                                ins = dve.tensor_scalar(score[:, lo:hi], r, w, None, ALU.mult)
                            else:
                                ins = dve.scalar_tensor_tensor(score[:, lo:hi], r, w, score[:, lo:hi], ALU.mult,
                                                               ALU.add)
                        ins.then_inc(relu_used, 1)
                        dve.wait_ge(relu_used, t.after(relu_used))
                    work, sel = area(S_W, PAIR), area(S_SEL, PAIR)
                    step(dve.tensor_tensor(work, score, area(S_ROPE + 128, PAIR), ALU.add))
                    for _ in range(TOPK // 8):
                        dve.max(rank[:, 0:8], work[:, 0:P])
                        step(dve.max(rank[:, 8:16], work[:, P:PAIR]))
                        dve.match_replace(work[:, 0:P], rank[:, 0:8], work[:, 0:P], TAKEN)
                        step(dve.match_replace(work[:, P:PAIR], rank[:, 8:16], work[:, P:PAIR], TAKEN))
                    step(dve.tensor_scalar(sel, work, TAKEN / 2, NEG, ALU.is_gt, ALU.mult))
                    attention(S_SM, sel, P ** -0.5)
                split(KD)
                layer_norm()

                turned_low()
                with t.loop(4, [(hi_done, 4)]):
                    split(4)
                p0, p1 = pad[:, X_P0:X_P0 + T], pad[:, X_P1:X_P1 + T]
                ca, cb = pad[:, X_CA:X_CA + T], pad[:, X_CB:X_CB + T]
                eq = pad[:, X_EQ:X_EQ + T].rearrange("p (k a) -> p k a", k=K16)
                val, best, idx_f, ab_f = rank[:, 0:32], rank[:, 32:48], rank[:, 48:80], rank[:, 80:112]
                idx_u, pos, ab_u = rank_u[:, 0:32], rank_u[:, 32:48], rank_u[:, 48:80]
                grid = lambda a: a.rearrange("p (a b) -> p a b", a=K16)
                row16 = lambda a: a.unsqueeze(1).broadcast_to([P, K16, K16])
                col16 = lambda a: a.unsqueeze(2).broadcast_to([P, K16, K16])
                i16 = cst[:, IOTA:IOTA + K16]

                def take(n):
                    dve.tensor_copy(p0, arena[:, bass.ds(n * T + E_S, T)]).then_inc(scores_taken, 1)
                    dve.wait_ge(scores_taken, t.after(scores_taken))

                def first8(n):
                    for f in range(2):
                        ins = dve.max(val[:, 16 * f:16 * f + 8], p0[:, NK * f:NK * f + NK])
                    step(ins)

                def first8_at(n):
                    for f in range(2):
                        v, row = val[:, 16 * f:16 * f + 8], slice(NK * f, NK * f + NK)
                        dve.max_index(idx_u[:, 16 * f:16 * f + 8], v, p0[:, row])
                        ins = dve.match_replace(p1[:, row], v, p0[:, row], TAKEN)
                    step(ins)

                def second8(n):
                    for f in range(2):
                        ins = dve.max(val[:, 16 * f + 8:16 * f + 16], p1[:, NK * f:NK * f + NK])
                    step(ins)

                def second8_at(n):
                    for f in range(2):
                        v, row = val[:, 16 * f + 8:16 * f + 16], slice(NK * f, NK * f + NK)
                        ins = dve.max_index(idx_u[:, 16 * f + 8:16 * f + 16], v, p1[:, row])
                    step(ins)
                    step(dve.tensor_tensor(grid(ca), col16(val[:, 0:16]), row16(val[:, 16:32]), ALU.add))

                def best8(n):
                    step(dve.max(best[:, 0:8], ca))
                    dve.tensor_copy(idx_f, idx_u)
                    dve.max_index(pos[:, 0:8], best[:, 0:8], ca)
                    step(dve.match_replace(cb, best[:, 0:8], ca, TAKEN))

                def best16(n):
                    step(dve.max(best[:, 8:16], cb))
                    dve.tensor_copy(pad[:, bass.ds(n * K16 + X_G, K16)], best)
                    step(dve.max_index(pos[:, 8:16], best[:, 8:16], cb))
                    dve.tensor_scalar(ab_u[:, 0:16], pos, 4, None, ALU.logical_shift_right)
                    step(dve.tensor_scalar(ab_u[:, 16:32], pos, 15, None, ALU.bitwise_and))
                    step(dve.tensor_copy(ab_f, ab_u))

                def decode(f, at):
                    def piece(n):
                        step(dve.tensor_tensor(eq, row16(i16), col16(ab_f[:, 16 * f:16 * f + 16]), ALU.is_equal))
                        step(dve.tensor_tensor(eq, eq, row16(idx_f[:, 16 * f:16 * f + 16]), ALU.mult))
                        step(dve.tensor_reduce(pad[:, bass.ds(n * K16 + at, K16)], eq, AX_X, ALU.add))
                    return piece

                pieces = [take, first8, first8_at, second8, second8_at, best8, best16, decode(0, X_I1)]
                with t.loop(NK // TURN, [(hi_done, TURN), (scores_taken, 1), (dve_step, TOPK_STEPS)]) as n:
                    for j in range(TURN):
                        split()
                        pieces[j](n)
                    decode(1, X_I2)(n)
                g3 = pad[:, X_G:X_G + T].rearrange("p (n k) -> p n k", k=K16)
                step(dve.tensor_copy(small[:, 32:48], g3[:, :, 0]))
                dve.tensor_tensor(g3, g3, small[:, 32:48].unsqueeze(2).broadcast_to([P, K16, K16]),
                                  ALU.subtract).then_inc(best_ready, 1)
                dve.wait_ge(gates_exp, t.after(gates_exp))
                step(dve.tensor_reduce(small[:, 48:64], g3, AX_X, ALU.add))
                step(dve.reciprocal(small[:, 64:80], small[:, 48:64]))
                dve.tensor_tensor(g3, g3, small[:, 64:80].unsqueeze(2).broadcast_to([P, K16, K16]),
                                  ALU.mult).then_inc(ranks_ready, 1)
                dve.wait_ge(hot_ready, t.after(hot_ready, 2))

                def one_hots(q, s):
                    for j in range(4):
                        ins = dve.tensor_scalar(pad[:, 1024 * s + 512 + NK * j:1024 * s + 512 + NK * (j + 1)], iota,
                                                hot[:, 1, bass.ds(q * 4 + j, 1)], hot[:, 2, bass.ds(q * 4 + j, 1)],
                                                ALU.is_equal, ALU.mult)
                    ins.then_inc(hot2_done, 1)

                def use_gates(q, s):
                    dve.wait_ge(gates_done, t.after(gates_done))
                    cols = keep[:, :, bass.ds(q * 4, 4)].rearrange("p c t -> p t c")
                    dve.tensor_tensor(cols, ps[:, 4 + s, :].rearrange("p (t c) -> p t c", t=4), cols,
                                      ALU.mult).then_inc(gates_used, 1)

                for s in range(2):
                    one_hots(s, s)
                with t.loop(T // 8 - 1, [(gates_done, 2)]) as n:
                    for s in range(2):
                        use_gates(n * 2 + s, s)
                        one_hots(n * 2 + (2 + s), s)
                for s in range(2):
                    use_gates(T // 4 - 2 + s, s)
                dve.wait_ge(gates_used, t.after(gates_used, T // 4))

                def chunk_low(c, j):
                    dve.wait_ge(eh_hi, t.after(eh_hi))
                    dve.tensor_tensor(act_lo[:, j, :], keep[:, bass.ds(c, 1), :].rearrange("p a t -> p (a t)"),
                                      act_hi[:, j, :].bitcast(F32), ALU.subtract).then_inc(eh_ready, 1)

                for j in range(KD):
                    chunk_low(j, j)
                with t.loop(NK // TURN - 1, [(hi_done, TURN), (eh_hi, TURN)]) as n:
                    for j in range(TURN):
                        split()
                        chunk_low(n * TURN + (TURN + j), j)
                split(TURN)
                layer_norm()

        @block.tensor
        def _(pe):
            t = Tally(pe)
            units = [0]

            def x_changed():
                pe.wait_ge(x_ready, t.after(x_ready, TB))

            def unit():
                pe.wait_ge(lo_done, t.after(lo_done))
                units[0] += 1
                return (units[0] - 1) % SPLIT

            def mm3(dst, lhs, rhs, first, last, **kw):
                pe.matmul(dst, lhs[0], rhs[0], start=first, stop=False, **kw)
                pe.matmul(dst, lhs[0], rhs[1], start=False, stop=False, **kw)
                return pe.matmul(dst, lhs[1], rhs[0], start=False, stop=last, **kw)

            def w(s, lo, n):
                return w_hi[:, s, lo:lo + n], w_lo[:, s, lo:lo + n]

            def a(k, lo=0, n=T):
                return act_hi[:, k, lo:lo + n], act_lo[:, k, lo:lo + n]

            def rows(set_, n_units, n=D, fresh=True, at=0):
                for k in range(n_units):
                    if fresh and k % 2 == 0:
                        pe.wait_ge(act_ready, t.after(act_ready))
                    s = unit()
                    for b in range(TB):
                        lhs = a(at + k, P * b, P)
                        for lo in range(0, n, 512):
                            m = min(512, n - lo)
                            ins = mm3(ps[:, 4 * set_ + 2 * b + lo // 512, 0:m], lhs, w(s, lo, m), k == 0,
                                      k == n_units - 1)
                    ins.then_inc(unit_used, 1)

            def turn(blocks, bank):
                for n, src in enumerate(blocks):
                    for b in range(TB):
                        ins = pe.transpose(ps[:, bank, T * n + P * b:T * n + P * b + P], src[:, b, :], ident)
                ins.then_inc(turned, 1)

            def turn_rows(src, banks):
                for n, bank in enumerate(banks):
                    turn([src[:, :, P * k:P * k + P] for k in (2 * n, 2 * n + 1)], bank)

            def norm():
                pe.wait_ge(rows_ready, t.after(rows_ready, TB))
                turn_rows(xn, range(4, 8))

            def open_acc():
                for b in range(4):
                    pe.matmul(ps[:, b, :], zero[0:1, :], zero[0:1, :].unsqueeze(1).broadcast_to([1, 4, P]),
                              start=True, stop=False, skip_group_check=True)

            def ffn():
                def features(dst, fresh=False):
                    s = unit()
                    for k in range(KD):
                        if fresh and k % 2 == 0:
                            pe.wait_ge(act_ready, t.after(act_ready))
                        ins = mm3(dst, w(s, P * k, P), a(k), k == 0, k == KD - 1)
                    return ins

                def gate_up(s, fresh=False):
                    features(ps[:, 4 + s, 0:T], fresh).then_inc(unit_used, 1)
                    features(ps[:, 4 + s, T:2 * T]).then_inc(unit_used, 1)

                def down(s, last=False):
                    pe.wait_ge(h_lo_ready, t.after(h_lo_ready))
                    slot = unit()
                    for b in range(TB):
                        lhs = h_hi[:, s, P * b:P * b + P], h_lo[:, s, P * b:P * b + P]
                        for half in range(2):
                            ins = mm3(ps[:, 2 * b + half, :], lhs, w(slot, 512 * half, 512), False, last,
                                      skip_group_check=True)
                    ins.then_inc(unit_used, 1)

                gate_up(0, True)
                open_acc()
                with t.loop(5, [(lo_done, 12), (h_lo_ready, 4)]):
                    for j in range(4):
                        gate_up((j + 1) % 2)
                        down(j % 2)
                gate_up(1)
                down(0)
                down(1, True)

            def stick_breaking():
                mask_tri = area(A_STICKC + PAIR, P)
                ones = area(A_STICKC + PAIR + P, P)
                pe.wait_ge(turned_kept, t.after(turned_kept, 8))
                pe.wait_ge(stick_in, 16)
                for p in range(N_PAIRS):
                    if p >= 4:
                        pe.wait_ge(z_used, t.after(z_used))
                    for h in range(2):
                        z, r = ps[:, 2 * (p % 4) + h, :], slice(64 * h, 64 * h + 64)
                        pe.matmul(z[:, 0:T], kT[r, p, 0:P], qT[r, p, 0:T], start=True, stop=True)
                        ins = pe.matmul(z[:, T:PAIR], kT[r, p, P:T], qT[r, p, P:T], start=True, stop=True)
                    ins.then_inc(z_done, 1)
                pe.wait_ge(z_used, t.after(z_used, 4))
                for p in range(N_PAIRS + 1):
                    if p < N_PAIRS:
                        pe.wait_ge(stay_ready, t.after(stay_ready))
                        if p >= 2:
                            pe.wait_ge(c_used, t.after(c_used))
                        for h in range(2):
                            c, s = ps[:, 2 * (p % 2) + h, :], stay[:, 2 * p + h, :]
                            pe.matmul(c[:, 0:PAIR], mask_tri, s, start=True, stop=False)
                            ins = pe.matmul(c[:, P:T], ones, s[:, T:PAIR], start=False, stop=True)
                        ins.then_inc(c_done, 1)
                    if p >= 1:
                        q = p - 1
                        pe.wait_ge(w_ready, t.after(w_ready))
                        if q >= 4:
                            pe.wait_ge(act_ready, t.after(act_ready))
                        for h in range(2):
                            o, e = ps[64 * h:64 * h + 64, 4 + q % 4, :], logw[:, 2 * q + h, :]
                            v = slice(HD * (2 * q + h), HD * (2 * q + h) + HD)
                            pe.matmul(o[:, 0:T], v_tok[:, 0, v], e[:, 0:T], start=True, stop=False)
                            ins = pe.matmul(o[:, P:T], v_tok[:, 1, v], e[:, T:PAIR], start=False, stop=True)
                        ins.then_inc(o_done, 1)
                t.skip(c_used, 2)
                pe.wait_ge(act_ready, t.after(act_ready, 4))

            def attention(sm_at, pt_at, terms):
                sm, pT = blk(sm_at, H2, PAIR), blk(pt_at, H2, PAIR)

                def scores(h):
                    if h >= 4:
                        pe.wait_ge(s_used, t.after(s_used))
                    s, both = ps[:, h % 4, :], terms(h)
                    for lo, q0, keys in ((0, 0, P), (P, P, T)):
                        for n, (k, q) in enumerate(both):
                            ins = pe.matmul(s[:, lo:lo + keys], q[:, q0:q0 + P], k[:, 0:keys], start=n == 0,
                                            stop=n == len(both) - 1)
                    ins.then_inc(s_done, 1)

                for h in range(4):
                    scores(h)
                for n in range(1, H2 + 2):
                    if n <= H2:
                        h = n - 1
                        pe.wait_ge(p_ready, t.after(p_ready))
                        if h >= 2:
                            pe.wait_ge(p_kept, t.after(p_kept))
                        for c in range(3):
                            ins = pe.transpose(ps[:, 4 + h % 2, P * c:P * c + P],
                                               sm[:, h, P * (0, 1, 2)[c]:P * (0, 1, 2)[c] + P], ident)
                        ins.then_inc(p_turned, 1)
                    if n >= 2:
                        h = n - 2
                        if h == 0 or h == H2 - 1:
                            pe.wait_ge(p_kept, t.after(p_kept))
                        if h >= 2:
                            pe.wait_ge(act_ready, t.after(act_ready))
                        o, v = ps[:, 6 + h % 2, :], slice(P * h, P * h + P)
                        pe.matmul(o[:, 0:T], v_tok[:, 0, v], pT[:, h, 0:T], start=True, stop=False)
                        pe.matmul(o[:, P:T], v_tok[:, 1, v], pT[:, h, T:PAIR], start=False,
                                  stop=True).then_inc(o_done, 1)
                    if n + 3 < H2:
                        scores(n + 3)
                t.skip(s_used, 4)
                pe.wait_ge(act_ready, t.after(act_ready, 2))

            pe.wait_ge(consts_in, 16)
            for i in range(DEPTH):
                norm()
                ffn()
                norm()
                if i == 0:
                    rows(0, KD)
                    rows(1, KD, fresh=False)
                    pe.wait_ge(acc_kept, t.after(acc_kept))
                    rows(0, KD, fresh=False)
                    pe.wait_ge(acc_kept, t.after(acc_kept))
                    pe.wait_ge(rows_ready, t.after(rows_ready))
                    turn_rows(q_tok, range(4, 8))
                    pe.wait_ge(acc_kept, t.after(acc_kept))
                    pe.wait_ge(rows_ready, t.after(rows_ready))
                    turn_rows(k_tok, range(4))
                    stick_breaking()
                    rows(0, KD, fresh=False)
                else:
                    rows(0, KD)
                    pe.wait_ge(acc_kept, t.after(acc_kept))
                    pe.wait_ge(pool_in, t.after(pool_in, 32))
                    mats = area(A_POOLC, 2048).rearrange("p (g b t) -> p g b t", g=4, b=TB)
                    for bank in range(4):
                        for n in range(2):
                            c = slice(P * (2 * bank + n), P * (2 * bank + n) + P)
                            dst = ps[:, 4 + bank, T * n:T * n + T]
                            pe.matmul(dst, q_tok[:, 0, c], mats[:, bank, 0, :], start=True, stop=False)
                            ins = pe.matmul(dst[:, P:T], q_tok[:, 1, c], mats[:, bank, 1, P:T], start=False,
                                            stop=True)
                        ins.then_inc(turned, 1)
                    pe.wait_ge(act_ready, t.after(act_ready, 4))
                    s0, s1 = unit(), unit()
                    for b in range(TB):
                        for g in range(4):
                            dst = ps[:, 2 * b + g // 2, T * (g % 2):T * (g % 2) + T]
                            mm3(dst, a(2 * g, P * b, P), w(s0, T * g, T), True, False)
                            ins = mm3(dst, a(2 * g + 1, P * b, P), w(s1, T * g, T), False, True)
                    ins.then_inc(unit_used, 2)
                norm()
                ffn()
                norm()
                rows(0, KD)
                sp_, s0, s1 = unit(), unit(), unit()
                for n, s in enumerate((s0, s1)):
                    for b in range(TB):
                        lhs = w(sp_, T * n + P * b, P)
                        for half in range(2):
                            ins = mm3(ps[:, 4 + 2 * b + half, :], lhs, w(s, 512 * half, 512), n == 0, n == 1)
                ins.then_inc(unit_used, 3)
                t.skip(acc_kept)
            t.skip(x_ready, TB * (4 * DEPTH - 1))
            for i in range(DEPTH):
                x_changed()
                turn_rows(x, range(4, 8))
                if i == 0:
                    c_tok, krd = tok(M_C, 704), tok(M_KRD, P)
                    rows(0, KD, 704)
                    pe.wait_ge(rows_ready, t.after(rows_ready))
                    c = [c_tok[:, :, P * k:P * k + P] for k in range(5)] + [krd]
                    for b in range(3):
                        turn(c[2 * b:2 * b + 2], 4 + b)
                    pe.wait_ge(act_ready, t.after(act_ready, 3))
                    s = unit()
                    for b in range(TB):
                        mm3(ps[:, b, :], a(0, P * b, P), w(s, 0, 512), True, False)
                        ins = mm3(ps[:, b, :], a(1, P * b, P), w(s, 512, 512), False, False)
                    ins.then_inc(unit_used, 1)
                    s = unit()
                    for b in range(TB):
                        ins = mm3(ps[:, b, :], a(2, P * b, P), w(s, 0, 512), False, True)
                    ins.then_inc(unit_used, 1)

                    def head_features(first_bank, depth, at):
                        for n in range(H2 * depth):
                            if n % 8 == 0:
                                if n:
                                    ins.then_inc(unit_used, 1)
                                s = unit()
                            h, r = divmod(n, depth)
                            ins = mm3(ps[:, first_bank + h // 2, T * (h % 2):T * (h % 2) + T],
                                      w(s, P * (n % 8), P), a(at + r), r == 0, r == depth - 1)
                        ins.then_inc(unit_used, 1)

                    head_features(4, 3, 0)
                    pe.wait_ge(acc_kept, t.after(acc_kept, 2))
                    head_features(0, 2, 3)
                    pe.wait_ge(acc_kept, t.after(acc_kept))
                    rows(1, 2, fresh=False, at=3)
                    pe.wait_ge(acc_kept, t.after(acc_kept))
                    pe.wait_ge(rows_ready, t.after(rows_ready))
                    turn_rows(tok(M_ROT, 512), range(2))
                    pe.wait_ge(turned_kept, t.after(turned_kept, 2))
                    pe.wait_ge(acc_kept, t.after(acc_kept))
                    qrT, krT = blk(M_QRT, 4), area(M_KRT, T)

                    def terms(h):
                        r = slice(64 * (h % 2), 64 * (h % 2) + 64)
                        return (kT[:, h, :], qT[:, h, :]), (krT[r, :], qrT[r, h // 2, :])

                    attention(M_SM, M_PT, terms)
                else:
                    rows(0, KD, 584)
                    rows(1, KD, fresh=False)
                    pe.wait_ge(acc_kept, t.after(acc_kept))
                    rows(0, KD, fresh=False)
                    pe.wait_ge(acc_kept, t.after(acc_kept))
                    rows(1, KD, fresh=False)
                    pe.wait_ge(acc_kept, t.after(acc_kept))
                    pe.wait_ge(rows_ready, t.after(rows_ready))
                    turn_rows(tok(S_IROT, 512), range(2))
                    turn([tok(S_KID, P)], 2)
                    pe.wait_ge(acc_kept, t.after(acc_kept))
                    pe.wait_ge(rows_ready, t.after(rows_ready))
                    turn_rows(tok(S_QROT, D), range(4, 8))
                    pe.wait_ge(turned_kept, t.after(turned_kept, 3))
                    pe.wait_ge(rows_ready, t.after(rows_ready))
                    turn_rows(tok(S_KROT, D), range(4))
                    pe.wait_ge(turned_kept, t.after(turned_kept, 8))
                    qiT, kiT = blk(S_IT, 4), area(S_KIT, T)
                    for h in range(H2):
                        if h >= 4:
                            pe.wait_ge(relu_done, t.after(relu_done))
                        r = slice(64 * (h % 2), 64 * (h % 2) + 64)
                        for lo, q0, keys in ((0, 0, P), (P, P, T)):
                            ins = pe.matmul(ps[:, 4 + h % 4, lo:lo + keys], qiT[r, h // 2, q0:q0 + P], kiT[r, 0:keys],
                                            start=True, stop=True)
                        ins.then_inc(i_done, 1)
                    t.skip(relu_done, 4)
                    attention(S_SM, S_PT, lambda h: ((kT[:, h, :], qT[:, h, :]),))
                rows(0, KD, fresh=False)

                x_changed()
                turn_rows(x, range(4, 8))
                pe.wait_ge(act_ready, t.after(act_ready, 4))

                def expert_features(bank):
                    s = unit()
                    for k in range(KD):
                        ins = mm3(ps[:, 4 + bank, 0:T], w(s, P * k, P), a(k), k == 0, k == KD - 1)
                    ins.then_inc(unit_used, 1)

                for j in range(4):
                    expert_features(j)
                with t.loop(3, [(lo_done, 4), (work_kept, 4)]):
                    for j in range(4):
                        pe.wait_ge(work_kept, t.after(work_kept))
                        expert_features(j)
                pe.wait_ge(work_kept, t.after(work_kept, 4))
                pe.wait_ge(subkeys_in, t.after(subkeys_in, 16))
                queries, keys = blk(E_Q, 16), blk(E_SK, 16, NK)
                for r in range(8):
                    if r >= 4:
                        pe.wait_ge(work_kept, t.after(work_kept))
                    for n in range(4):
                        hh = 4 * (r % 4) + n
                        ins = pe.matmul(ps[:, 4 + r % 4, NK * n:NK * n + NK], queries[:, hh, P * (r // 4):P * (r // 4) + P],
                                        keys[:, hh, :], start=True, stop=True)
                    ins.then_inc(scores_done, 1)
                with t.loop(NK // TURN, [(lo_done, TURN), (work_kept, TURN)]):
                    for j in range(TURN):
                        pe.wait_ge(work_kept, t.after(work_kept))
                        expert_features(j % 4)
                pe.wait_ge(work_kept, t.after(work_kept, 4))
                pe.wait_ge(ranks_ready, t.after(ranks_ready))
                ranks = pad[:, X_I1:X_I1 + 3 * T].rearrange("p (n b c) -> p n b c", n=3, b=TB)
                turn([ranks[:, 0], ranks[:, 1]], 4)
                turn([ranks[:, 2]], 5)

                def gate_matrices(s):
                    pe.wait_ge(hot1_done, t.after(hot1_done))
                    pe.wait_ge(hot2_done, t.after(hot2_done))
                    for j in range(4):
                        ins = pe.matmul(ps[:, 4 + s, NK * j:NK * j + NK], pad[:, 1024 * s + NK * j:1024 * s + NK * (j + 1)],
                                        pad[:, 1024 * s + 512 + NK * j:1024 * s + 512 + NK * (j + 1)],
                                        start=True, stop=True)
                    ins.then_inc(gates_done, 1)

                for s in range(2):
                    gate_matrices(s)
                with t.loop(T // 8 - 1, [(hot1_done, 2), (hot2_done, 2), (gates_used, 2)]):
                    for s in range(2):
                        pe.wait_ge(gates_used, t.after(gates_used))
                        gate_matrices(s)
                pe.wait_ge(gates_used, t.after(gates_used, 2))

                open_acc()

                def expert_down(j, last=False):
                    pe.wait_ge(eh_ready, t.after(eh_ready))
                    s = unit()
                    for b in range(TB):
                        for half in range(2):
                            ins = mm3(ps[:, 2 * b + half, :], a(j, P * b, P), w(s, 512 * half, 512), False, last,
                                      skip_group_check=True)
                    ins.then_inc(unit_used, 1)

                with t.loop(NK // TURN - 1, [(lo_done, TURN), (eh_ready, TURN)]):
                    for j in range(TURN):
                        expert_down(j)
                for j in range(TURN):
                    expert_down(j, j == TURN - 1)


def _columns(w, chunk=P):
    k, n = w.shape
    return w.reshape(k // P, P, n // chunk, chunk).transpose(2, 1, 0, 3).reshape(n // chunk, P, -1)


def _blocks(w):
    return w.reshape(-1, P, w.shape[1])


def _padded(units):
    out = np.zeros(units.shape[:2] + (UNIT,), np.float32)
    out[:, :, :units.shape[2]] = units
    return out


def _heads(w, depth):
    a = w.reshape(depth, P, H2, P).transpose(1, 2, 0, 3).reshape(P, -1)
    return a.reshape(P, -1, UNIT).transpose(1, 0, 2)


def _stream(v):
    parts = []

    def ffn(gu, down):
        g, d = _columns(gu), _blocks(down)
        out = np.empty((3 * FC, P, UNIT), np.float32)
        order = [("g", 0), ("u", 0)]
        for c in range(1, FC):
            order += [("g", c), ("u", c), ("d", c - 1)]
        order += [("d", FC - 1)]
        for n, (kind, c) in enumerate(order):
            out[n] = g[c] if kind == "g" else g[FC + c] if kind == "u" else d[c]
        parts.append(out)

    for i in range(DEPTH):
        ffn(v["w_ffn1_gu"][i], v["w_ffn1_down"][i])
        if i == 0:
            qkv = v["w_qkv"][0]
            parts.extend(_blocks(qkv[:, D * n:D * n + D]) for n in range(3))
            parts.append(_blocks(v["w_o"][0]))
        else:
            parts.append(_blocks(v["w_pool_in"][0]))
            g = v["w_pool_grp"][0].reshape(4, 2, P, T)
            parts.append(g.transpose(1, 2, 0, 3).reshape(2, P, UNIT))
        ffn(v["w_ffn2_gu"][i], v["w_ffn2_down"][i])
        parts.append(_blocks(v["w_ple_gate"][i]))
        parts.append(_padded(v["p"][i, 0].T.reshape(2, P, T).transpose(1, 0, 2).reshape(1, P, 2 * T)))
        parts.append(_blocks(v["w_ple_proj"][i]))

    def peer(i):
        parts.append(_columns(v["peer_w_q_2"][i]))
        down = v["peer_w_down_2"][i].reshape(NK, NK, KD, P)
        parts.append(down.transpose(1, 3, 2, 0).reshape(NK, P, UNIT))
        parts.append(v["peer_w_up_2"][i].reshape(NK, NK, D).transpose(1, 0, 2))

    parts.append(_padded(_blocks(v["mla_w_in_2"][0])))
    uq, ukv = v["mla_w_uq_2"][0], v["mla_w_ukv_2"][0]
    rope = uq[:, :, P:].reshape(3, P, 512).transpose(1, 0, 2).reshape(P, 3 * 512)
    parts.append(rope[:, :UNIT][None])
    parts.append(_padded(rope[:, UNIT:][None]))
    parts.append(_heads(uq[:, :, :P], 3))
    parts.append(_heads(ukv[:, :, :P], 2))
    parts.append(_blocks(ukv[:, :, P:].reshape(KV_RANK, D)))
    parts.append(_blocks(v["mla_w_o_2"][0]))
    peer(0)
    w_in = v["dsa_w_in_2"][0]
    parts.append(_padded(_blocks(w_in[:, 3 * D:])))
    parts.extend(_blocks(w_in[:, D * n:D * n + D]) for n in range(3))
    parts.append(_blocks(v["dsa_w_o_2"][0]))
    peer(1)
    parts.append(np.zeros((N_UNITS - sum(len(a) for a in parts), P, UNIT), np.float32))
    return np.concatenate(parts)


def _consts(v):
    c = np.zeros((P, N_CONST), np.float32)
    c[:, IDENT:IDENT + P] = np.eye(P)
    c[:, IOTA:IOTA + P] = np.arange(P)
    c[:, HALF] = -0.5
    c[:, ONE] = 1.0
    c[:, QG] = np.tile(v["q_norm"][0], 2)
    c[:, KG] = np.tile(v["k_norm"][0], 2)
    c[:, G_MLA:G_MLA + 3] = v["mla_q_norm_2"][0].reshape(3, P).T
    c[:, G_MLA + 3:G_MLA + 5] = v["mla_kv_norm_2"][0].reshape(2, P).T
    for i in range(DEPTH):
        for n, name in enumerate(("norm_ffn1", "norm_mix", "norm_ffn2", "norm_ple")):
            at = G_NORM + KD * (4 * i + n)
            c[:, at:at + KD] = v[name][i].reshape(KD, P).T
    return c


def _shape_tables():
    k, q = np.arange(P)[:, None], np.arange(T)[None, :]
    stick = np.zeros((P, STICK_COLS), np.float32)
    stick[:, 0:T] = k < q
    stick[:, T:PAIR] = k < q[:, :P]
    stick[:, PAIR:PAIR + P] = np.arange(P)[:, None] > np.arange(P)[None, :]
    stick[:, PAIR + P:] = 1.0
    pool = np.zeros((4, T, T), np.float32)
    for g, w in enumerate(WINDOWS):
        for s in range(T):
            n = min(s + 1, w)
            pool[g, s + 1 - n:s + 1, s] = np.float32(1.0) / np.float32(n)
            pool[g, s, s] -= 1.0
    pool = pool.reshape(4, TB, P, T).transpose(2, 0, 1, 3).reshape(P, -1)
    rope = np.zeros((P, ROPE_COLS), np.float32)
    for at, dim in ((0, ROPE), (512, P)):
        inv = np.float32(10000.0) ** (-np.arange(0, dim, 2, dtype=np.float32) / np.float32(dim))
        ang = np.arange(T, dtype=np.float32)[:, None] * inv[None, :].astype(np.float32)
        half = dim // 2
        for n, f in enumerate((np.cos, np.sin)):
            tab = f(ang).astype(np.float32).reshape(TB, P, half).transpose(1, 0, 2).reshape(P, TB * half)
            rope[:, at + n * TB * half:at + (n + 1) * TB * half] = tab
    chunk = np.arange(T) // 64
    mask = np.where(chunk[None, :] <= chunk[:, None], 0.0, NEG)
    rope[:, 128:256] = mask[0:P, 0:P]
    rope[:, 256:512] = mask[P:T, :]
    return stick, pool, rope


def kernel(**inputs):
    import concourse.bacc as bacc
    from concourse.bass_utils import run_bass_kernel_spmd

    v = {name: np.asarray(a) for name, a in inputs.items()}
    stick, pool, rope = _shape_tables()
    ln = np.stack([v["ln_gain_2"], v["ln_bias_2"]], axis=2).reshape(2 * DEPTH, 1, 2 * D)
    arrays = {
        "stream": _stream(v),
        "x": np.ascontiguousarray(v["x"][0]),
        "consts": _consts(v),
        "stick": stick,
        "pool": pool,
        "scale": np.ascontiguousarray(np.broadcast_to(v["pool_scale"], (P, D))),
        "rope": rope,
        "ln": np.ascontiguousarray(np.broadcast_to(ln, (2 * DEPTH, P, 2 * D))),
        "subkeys": np.ascontiguousarray(
            v["peer_sub_keys_2"].transpose(0, 4, 2, 1, 3).reshape(DEPTH, P, 2048)),
    }
    nc = bacc.Bacc("TRN2", target_bir_lowering=False, num_devices=1)
    args = [nc.dram_tensor(f"in_{name}", a.shape, mybir.dt.from_np(a.dtype), kind="ExternalInput").ap()
            for name, a in arrays.items()]
    out = nc.dram_tensor("out", (T, D), F32, kind="ExternalOutput").ap()
    program(nc, *args, out)
    r = run_bass_kernel_spmd(nc, [{f"in_{name}": a for name, a in arrays.items()}], core_ids=[0])
    return r.results[0]["out"].reshape(1, T, D)
```

```python
import numpy as np
from contextlib import ExitStack, contextmanager

import concourse.bass as bass
from concourse import mybir

F32 = mybir.dt.float32
F32R = mybir.dt.float32r
U32 = mybir.dt.uint32
ALU = mybir.AluOpType
ACT = mybir.ActivationFunctionType
AX_X = mybir.AxisListType.X

P = 128
D = 1024
T = 256
TB = T // P
KD = D // P
DEPTH = 2
D_FF = 2816
FC = D_FF // P
HEADS, HD = 16, 64
WINDOWS = (2, 4, 8, 16)
EPS, LN_EPS = 1e-6, 1e-5
ALPHA = (2 * DEPTH) ** 0.25
Q_RANK, KV_RANK, ROPE = 384, 256, 64
H2 = 8
IDX = 64
KEEP = min(256, T // 4)
NK = 128
K16 = 16
UNIT = 1024
RAW, SPLIT = 6, 4
PAIR = 384
STICK_GROUP = 2
NEG = -1e30
TAKEN = -3e38
TURN = 12
RING = 6
HOT = 4

IDENT, IOTA, HALF, ONE, QG, KG, G_MLA = 0, 128, 256, 257, 258, 259, 260
G_NORM = 265
G_LN = G_NORM + 8 * KD
N_CONST = G_LN + 2 * DEPTH * 2 * KD

ARENA = NK * T
A_Q, A_K, A_V, A_QT, A_KT = 0, 2048, 4096, 6144, 8192
A_STAY, A_LOGW = 10240, 16384
A_LN, A_SOFT = 22528, 25600
A_STICKC = 27136
A_FFN = 24576
A_XN, A_SQ = 28672, 30720
A_POOLC, A_SCALE = 10240, 12288
M_C, M_QR, M_ROT, M_QRT, M_KRD, M_KRT, M_RA, M_RB, M_SM, M_PT, M_ROPE = (
    0, 2048, 3072, 10240, 11264, 11520, 12288, 13312, 16384, 19456, 27136)
S_I, S_IROT, S_IT, S_KID, S_KIT, S_RA, S_RB, S_SM, S_PT, S_QROT, S_KROT, S_IDX, S_ROPE, S_RELU, S_W, S_SEL = (
    12288, 13568, 10240, 11264, 11520, 14592, 16640, 18688, 21760, 24832, 18688, 26880, 27648, 30720,
    31488, 32256)
E_Q, E_SK, E_S = 0, 4096, 28672
X_P0, X_P1, X_CA, X_CB, X_I1, X_I2, X_G = 0, 256, 512, 768, 1024, 1280, 1536
STICK_COLS, ROPE_COLS = PAIR + 2 * P, 768


def unit_plan():
    ffn = 3 * FC
    plan = []
    for i in range(DEPTH):
        plan += [("ffn", ffn)]
        plan += [("qkv", 3 * KD), ("wo", KD)] if i == 0 else [("pool", KD), ("grp", 2)]
        plan += [("ffn", ffn), ("gate", KD), ("ple", 3)]
    plan += [("mla_in", KD), ("mla_qr", 2), ("mla_qn", 3), ("mla_kn", 2), ("mla_v", 2), ("mla_o", KD)]
    plan += [("peer_q", 16), ("down", NK), ("up", NK)]
    plan += [("dsa_in", 4 * KD), ("dsa_o", KD)]
    plan += [("peer_q", 16), ("down", NK), ("up", NK)]
    return plan


SPREAD = 8
PAIRS = 3
POOL_HOT, ACT_HOT = 2, 2
TOPK_STEPS = 14
KEPT_MLA = 3 + 1 + DEPTH + 1
N_UNITS = sum(n for _, n in unit_plan()) + SPLIT
N_UNITS += N_UNITS % RAW


class Tally:

    def __init__(self, eng, start=()):
        self.eng, self.at, self.step, self.i = eng, dict(start), {}, None

    def value(self, sem):
        v = self.at.get(sem.name, 0)
        return v if self.i is None else v + self.step.get(sem.name, 0) * self.i

    def after(self, sem, n=1):
        self.at[sem.name] = self.at.get(sem.name, 0) + n
        return self.value(sem)

    skip = after

    @contextmanager
    def loop(self, turns, steps):
        base = dict(self.at)
        self.step = {s.name: n for s, n in steps}
        with self.eng.Fori(0, turns) as i:
            self.i = i
            yield i
        for name in set(self.at) | set(self.step):
            grew = self.at.get(name, 0) - base.get(name, 0)
            assert grew == self.step.get(name, 0), (name, grew, self.step.get(name, 0))
            self.at[name] = base.get(name, 0) + grew * turns
        self.i, self.step = None, {}


def program(nc, stream, x_in_dram, consts, stickc, poolc, scalec, ropec, lnc, subkeys, out):
    with ExitStack() as ctx:
        base = -(-nc.sbuf_base // 32) * 32
        hots_at = base + 4 * ARENA
        raw_at = hots_at + 4 * 2 * KD * T
        arena = ctx.enter_context(nc.sbuf_tensor("arena", [P, ARENA], F32))
        first_hot = ctx.enter_context(nc.sbuf_tensor("first_hot", [P, HOT, 4, NK], F32))
        second_hot = ctx.enter_context(nc.sbuf_tensor("second_hot", [P, HOT, 4, NK], F32))
        raw = ctx.enter_context(nc.sbuf_tensor("raw", [P, RAW, UNIT], F32))

        def in_place(name, shape, offset):
            return nc.alloc_sbuf_tensor_at(name, shape, F32R, offset=offset)

        act_hi = in_place("act_hi", [P, KD, T], hots_at)
        act_lo = in_place("act_lo", [P, KD, T], hots_at + 4 * KD * T)
        w_lo = in_place("w_lo", [P, RAW, UNIT], raw_at)
        h_hi = in_place("h_hi", [P, 2, T], base + 4 * (A_FFN + 4 * T))
        h_lo = in_place("h_lo", [P, 2, T], base + 4 * (A_FFN + 6 * T))

        def sb(name, shape, dt=F32):
            return ctx.enter_context(nc.sbuf_tensor(name, shape, dt))

        def sem(name):
            return ctx.enter_context(nc.semaphore(name))

        x = sb("x", [P, TB, D])
        w_hi = sb("w_hi", [P, SPLIT, UNIT], F32R)
        cst = sb("cst", [P, N_CONST])
        zero = sb("zero", [1, P], F32R)
        small = sb("small", [P, 96])
        stats = sb("stats", [P, 48])
        pad = sb("pad", [P, 2048])
        hot = sb("hot", [P, 4, T])
        rank = sb("rank", [P, 112])
        rank_u = sb("rank_u", [P, 80], U32)
        ps = ctx.enter_context(nc.psum_tensor("ps", [P, 8, 512], F32))

        landed = [sem(f"landed{s}") for s in range(RAW)]
        hi_done = sem("hi_done")
        lo_done = sem("lo_done")
        unit_used = sem("unit_used")
        x_in, consts_in, stick_in, pool_in, rope_in, ln_in, subkeys_in = (
            sem(n) for n in ("x_in", "consts_in", "stick_in", "pool_in", "rope_in", "ln_in", "subkeys_in"))
        act_step = sem("act_step")
        dve_step = sem("dve_step")
        pool_step = sem("pool_step")
        pool_past = sem("pool_past")
        x_ready = sem("x_ready")
        stat_ready = sem("stat_ready")
        mean_ready = sem("mean_ready")
        var_ready = sem("var_ready")
        rstd_ready = sem("rstd_ready")
        rows_ready = sem("rows_ready")
        turned = sem("turned")
        turned_hi = sem("turned_hi")
        act_ready = sem("act_ready")
        turned_kept = sem("turned_kept")
        acc_kept = sem("acc_kept")
        silu_done = sem("silu_done")
        h_ready = sem("h_ready")
        h_hi_ready = sem("h_hi_ready")
        h_lo_ready = sem("h_lo_ready")
        z_done = sem("z_done")
        ln_done = sem("ln_done")
        soft_done = sem("soft_done")
        z_used = sem("z_used")
        stay_ready = sem("stay_ready")
        c_done = sem("c_done")
        c_used = sem("c_used")
        w_exp = sem("w_exp")
        w_ready = sem("w_ready")
        o_done = sem("o_done")
        o_hi = sem("o_hi")
        i_done = sem("i_done")
        relu_done = sem("relu_done")
        relu_used = sem("relu_used")
        s_done = sem("s_done")
        s_used = sem("s_used")
        max_ready = sem("max_ready")
        e_done = sem("e_done")
        p_ready = sem("p_ready")
        p_turned = sem("p_turned")
        p_kept = sem("p_kept")
        scores_done = sem("scores_done")
        work_kept = sem("work_kept")
        scores_taken = sem("scores_taken")
        best_ready = sem("best_ready")
        gates_exp = sem("gates_exp")
        ranks_ready = sem("ranks_ready")
        hot_ready = sem("hot_ready")
        hot1_done = sem("hot1_done")
        hot2_done = sem("hot2_done")
        hot3_done = sem("hot3_done")
        gates_done = sem("gates_done")
        gates_used = sem("gates_used")
        eh_hi = sem("eh_hi")
        eh_ready = sem("eh_ready")
        out_done = sem("out_done")

        ident = cst[:, IDENT:IDENT + P]
        iota = cst[:, IOTA:IOTA + P]

        def area(at, n):
            return arena[:, at:at + n]

        def tok(at, n):
            return area(at, TB * n).rearrange("p (b n) -> p b n", b=TB)

        def blk(at, n, w=T):
            return area(at, n * w).rearrange("p (k t) -> p k t", k=n)

        def acc(s, n=D):
            return ps[:, 4 * s:4 * s + 4, :].rearrange("p (b h) c -> p b (h c)", b=TB)[:, :, 0:n]

        diag, sq = tok(A_XN, P), tok(A_SQ, D)
        xT = blk(A_XN, KD)
        q_tok, k_tok, v_tok = tok(A_Q, D), tok(A_K, D), tok(A_V, D)
        qT, kT = blk(A_QT, KD), blk(A_KT, KD)
        silu, prod = blk(A_FFN, 2), blk(A_FFN + 2 * T, 2)
        keep = arena[:, :].rearrange("p (c t) -> p c t", t=T)
        stay, logw = blk(A_STAY, HEADS, PAIR), blk(A_LOGW, HEADS, PAIR)
        sigma = tok(A_Q, D)
        ln_g, ln_b = pad[:, 0:D], pad[:, D:2 * D]
        N_PAIRS = HEADS // 2
        near = pad[:, 0:HOT * 4 * NK].rearrange("p (s n) -> p s n", n=NK)
        block = ctx.enter_context(nc.Block())

        @block.sync
        def _(sp):
            sp.dma_start(x[:, :, :], x_in_dram.rearrange("(b p) d -> p b d", b=TB)).then_inc(x_in, 16)
            for u in range(RAW):
                sp.dma_start(raw[:, u, :], stream[u]).then_inc(landed[u], 16)
            with sp.Fori(1, N_UNITS // RAW) as i:
                for s in range(RAW):
                    sp.wait_ge(unit_used, i * RAW + (s - RAW + 1))
                    sp.dma_start(raw[:, s, :], stream[i * RAW + s]).then_inc(landed[s], 16)
            sp.wait_ge(x_ready, TB * (4 * DEPTH + 2 * DEPTH))
            sp.dma_start(out.rearrange("(b p) d -> p b d", b=TB), x[:, :, :]).then_inc(out_done, 16)
            sp.wait_ge(out_done, 16)

        @block.gpsimd
        def _(pool):
            t = Tally(pool)
            pool.dma_start(cst[:, :], consts).then_inc(consts_in, 16)
            pool.wait_ge(consts_in, 16)

            def power(src, dst, n):
                pool.wait_ge(var_ready, t.after(var_ready))
                pool.tensor_tensor(small[:, dst:dst + n], small[:, src:src + n],
                                   cst[:, HALF:HALF + 1].broadcast_to([P, n]), ALU.pow).then_inc(rstd_ready, 1)

            def norm():
                for b in range(TB):
                    power(b, 16 + b, 1)

            def x_changed():
                pool.wait_ge(x_ready, t.after(x_ready, TB))

            def stick_breaking():
                m = area(A_STICKC, PAIR).unsqueeze(1).broadcast_to([P, 2, PAIR])
                soft = blk(A_SOFT, 4, PAIR)
                for p in range(N_PAIRS):
                    pool.wait_ge(soft_done, t.after(soft_done))
                    pool.tensor_tensor(stay[:, 2 * p:2 * p + 2, :], soft[:, 2 * (p % 2):2 * (p % 2) + 2, :], m,
                                       ALU.mult).then_inc(stay_ready, 1)
                for p in range(N_PAIRS):
                    pool.wait_ge(w_exp, t.after(w_exp))
                    w = logw[:, 2 * p:2 * p + 2, :]
                    pool.tensor_tensor(w, w, m, ALU.mult).then_inc(w_ready, 1)

            for i in range(DEPTH):
                norm()
                x_changed()
                norm()
                if i == 0:
                    pool.dma_start(area(A_STICKC, STICK_COLS), stickc).then_inc(stick_in, 16)
                else:
                    pool.dma_start(area(A_POOLC, 2048), poolc).then_inc(pool_in, 16)
                    pool.dma_start(area(A_SCALE, D), scalec).then_inc(pool_in, 16)
                if i == 0:
                    power(32, 64, 32)
                    power(32, 64, 32)
                    pool.wait_ge(stick_in, t.after(stick_in, 16))
                    stick_breaking()
                x_changed()
                norm()
                x_changed()
                norm()
                x_changed()
            for i in range(DEPTH):
                at = M_ROPE if i == 0 else S_ROPE
                pool.dma_start(area(at, ROPE_COLS), ropec).then_inc(rope_in, 16)
                pool.dma_start(pad[:, :], lnc[2 * i]).then_inc(ln_in, 16)
                if i == 0:
                    power(0, 16, 4)
                norm()
                x_changed()
                pool.dma_start(area(E_SK, 2048), subkeys[i]).then_inc(subkeys_in, 16)
                pool.wait_ge(hot_ready, t.after(hot_ready, 3))

                first = small[:, 80:80 + 4 * HOT]

                def indices(n):
                    pool.tensor_copy(first, hot[:, 0, bass.ds(n * 4 * HOT, 4 * HOT)]).then_inc(pool_step, 1)
                    pool.wait_ge(pool_step, t.after(pool_step))
                    pool.sem_inc(pool_past, 1)

                def one_hots(s):
                    for j in range(POOL_HOT):
                        ins = pool.tensor_scalar(first_hot[:, s, j, :], iota, first[:, 4 * s + j:4 * s + j + 1],
                                                 None, ALU.is_equal)
                    ins.then_inc(hot1_done, 1)

                indices(0)
                for s in range(HOT):
                    one_hots(s)
                with t.loop(T // (4 * HOT) - 1, [(gates_done, HOT), (pool_step, 1), (hot1_done, HOT)]) as n:
                    pool.wait_ge(hot1_done, t.after(hot1_done, HOT))
                    indices(n + 1)
                    for s in range(HOT):
                        pool.wait_ge(gates_done, t.after(gates_done))
                        pool.sem_inc(pool_past, 1)
                        one_hots(s)
                t.skip(gates_done, HOT)
                t.skip(hot1_done, HOT)
                pool.wait_ge(gates_used, t.after(gates_used, T // 4))
                pool.dma_start(pad[:, :], lnc[2 * i + 1]).then_inc(ln_in, 16)
                norm()
                x_changed()

        @block.scalar
        def _(act):
            t = Tally(act, {unit_used.name: -SPLIT})
            units = [0]

            def step(ins):
                ins.then_inc(act_step, 1)
                act.wait_ge(act_step, t.after(act_step))

            def split(n=1):
                for _ in range(n):
                    u = units[0]
                    units[0] += 1
                    act.wait_ge(landed[u % RAW], t.after(landed[u % RAW], 16))
                    free = t.after(unit_used)
                    if u >= SPLIT:
                        act.wait_ge(unit_used, free)
                    act.activation(w_hi[:, u % SPLIT, :], raw[:, u % RAW, :], ACT.Copy).then_inc(hi_done, 1)

            def unit_steps(n):
                return [(landed[s], 16 * n // RAW) for s in range(RAW)] + [(unit_used, n)]

            def squares(pending=0, first=False):
                for b in range(TB):
                    if first:
                        act.wait_ge(x_in, 16)
                    else:
                        act.wait_ge(x_ready, t.after(x_ready))
                    act.activation(sq[:, b, :], x[:, b, :], ACT.Square,
                                   accum_out=small[:, 8 + b:9 + b]).then_inc(stat_ready, 1)
                    if b < pending:
                        split()

            def turned_high(gain=None, banks=4):
                for b in range(banks):
                    act.wait_ge(turned, t.after(turned))
                    if gain is None:
                        ins = act.activation(act_hi[:, 2 * b:2 * b + 2, :], ps[:, 4 + b, :], ACT.Copy)
                    else:
                        for k in (2 * b, 2 * b + 1):
                            ins = act.activation(act_hi[:, k, :], ps[:, 4 + b, (k % 2) * T:(k % 2) * T + T],
                                                 ACT.Copy, scale=cst[:, gain + k:gain + k + 1])
                    ins.then_inc(turned_hi, 1)

            def turned_ln(n):
                for b in range(4):
                    act.wait_ge(turned, t.after(turned))
                    for k in (2 * b, 2 * b + 1):
                        g = G_LN + 2 * KD * n + k
                        ins = act.activation(xT[:, k, :], ps[:, 4 + b, (k % 2) * T:(k % 2) * T + T], ACT.Identity,
                                             scale=cst[:, g:g + 1], bias=cst[:, g + KD:g + KD + 1])
                    step(ins)
                    act.activation(act_hi[:, 2 * b:2 * b + 2, :], xT[:, 2 * b:2 * b + 2, :],
                                   ACT.Copy).then_inc(turned_hi, 1)

            def keep_turned(dst, banks, gain=1.0):
                for n, b in enumerate(banks):
                    act.wait_ge(turned, t.after(turned))
                    act.activation(dst[:, 512 * n:512 * n + 512], ps[:, b, :], ACT.Copy,
                                   scale=gain).then_inc(turned_kept, 1)

            def product_done():
                act.wait_ge(unit_used, t.value(unit_used))

            def keep_acc(dst, s, n=D, func=ACT.Copy):
                product_done()
                for b in range(TB):
                    ins = act.activation(dst[:, b, :], acc(s, n)[:, b, :], func)
                ins.then_inc(acc_kept, 1)

            def norm(g, pending=0, first=False):
                squares(pending, first)
                turned_high(G_NORM + KD * g)

            def ffn():
                def chunk(s, units_after=1):
                    act.wait_ge(unit_used, t.value(unit_used) + units_after)
                    act.activation(silu[:, s, :], ps[:, 4 + s, 0:T], ACT.Silu).then_inc(silu_done, 1)
                    split()
                    act.wait_ge(h_ready, t.after(h_ready))
                    act.activation(h_hi[:, s, :], prod[:, s, :], ACT.Copy).then_inc(h_hi_ready, 1)
                    split(2)

                chunk(0, 2)
                with t.loop(5, [(h_ready, 4)] + unit_steps(12)):
                    for j in range(4):
                        chunk((j + 1) % 2)
                chunk(1)

            def stick_breaking():
                ln = blk(A_LN, 8, PAIR)
                for first in range(0, N_PAIRS, STICK_GROUP):
                    group = range(first, first + STICK_GROUP)
                    for p in group:
                        act.wait_ge(z_done, t.after(z_done))
                        m = ln[:, 2 * (p % 4):2 * (p % 4) + 2, :]
                        step(act.activation(m, ps[:, 2 + 2 * (p % 3):4 + 2 * (p % 3), 0:PAIR], ACT.Abs))
                        ins = act.activation(m, m, ACT.Exp, scale=-1.0)
                    step(ins)
                    for p in group:
                        m = ln[:, 2 * (p % 4):2 * (p % 4) + 2, :]
                        act.activation(m, m, ACT.Ln, bias=cst[:, ONE:ONE + 1]).then_inc(ln_done, 1)
                for p in range(N_PAIRS + 1):
                    if p < N_PAIRS:
                        act.wait_ge(c_used, t.after(c_used))
                        w = logw[:, 2 * p:2 * p + 2, :]
                        act.activation(w, w, ACT.Exp).then_inc(w_exp, 1)
                    if p >= 1:
                        heads_high(p - 1, 4 + (p - 1) % 4)

            def heads_high(k, bank):
                act.wait_ge(o_done, t.after(o_done))
                act.activation(act_hi[:, k, :], ps[:, bank, 0:T], ACT.Copy).then_inc(o_hi, 1)

            def attention(sm_at, pt_at):
                sm, pT = blk(sm_at, H2, PAIR), blk(pt_at, H2, PAIR)
                for n in range(H2 + 2):
                    if n < H2:
                        act.wait_ge(max_ready, t.after(max_ready))
                        for b, (lo, hi) in enumerate(((0, P), (P, PAIR))):
                            ins = act.activation(sm[:, n, lo:hi], sm[:, n, lo:hi], ACT.Exp,
                                                 bias=stats[:, 2 * n + b:2 * n + b + 1],
                                                 accum_out=stats[:, 16 + 2 * n + b:17 + 2 * n + b])
                        ins.then_inc(e_done, 1)
                    if 1 <= n <= H2:
                        act.wait_ge(p_turned, t.after(p_turned))
                        act.activation(pT[:, n - 1, :], ps[:, 4 + (n - 1) % 2, 0:PAIR], ACT.Copy).then_inc(p_kept, 1)
                    if n >= 2:
                        heads_high(n - 2, 6 + n % 2)

            def layer_norm():
                for b in range(TB):
                    act.wait_ge(mean_ready, t.after(mean_ready))
                    act.activation(sq[:, b, :], x[:, b, :], ACT.Square,
                                   bias=small[:, 12 + b:13 + b],
                                   accum_out=small[:, 10 + b:11 + b]).then_inc(stat_ready, 1)

            for i in range(DEPTH):
                if i == 0:
                    squares(0, True)
                    split(SPLIT)
                    act.wait_ge(consts_in, 16)
                    turned_high(G_NORM)
                else:
                    norm(4 * i, 2)
                ffn()
                norm(4 * i + 1)
                if i == 0:
                    split(KD)
                    keep_acc(q_tok, 0)
                    split(KD)
                    keep_acc(k_tok, 1)
                    split(KD)
                    keep_acc(v_tok, 0)
                    keep_turned(area(A_QT, 2048), range(4, 8), cst[:, QG:QG + 1])
                    keep_turned(area(A_KT, 2048), range(4), cst[:, KG:KG + 1])
                    stick_breaking()
                    split(KD)
                else:
                    split(KD)
                    keep_acc(q_tok, 0)
                    turned_high()
                    split()
                norm(4 * i + 2, i)
                ffn()
                norm(4 * i + 3)
                split(KD)
                keep_acc(sigma, 0, D, ACT.Sigmoid)
                split(1 if i == 0 else 3)
            t.skip(x_ready, TB)
            for i in range(DEPTH):
                if i == 0:
                    turned_high()
                else:
                    turned_ln(1)
                if i == 0:
                    c_tok = tok(M_C, 704)
                    split(KD)
                    product_done()
                    for b in range(TB):
                        ins = act.activation(c_tok[:, b, :], acc(0, 704)[:, b, :], ACT.Copy)
                    ins.then_inc(acc_kept, 1)
                    act.wait_ge(acc_kept, KEPT_MLA)
                    for c, (lo, hi) in enumerate(((0, Q_RANK), (Q_RANK, Q_RANK + KV_RANK))):
                        for b in range(TB):
                            ins = act.activation(sq[:, b, lo:hi], c_tok[:, b, lo:hi], ACT.Square,
                                                 accum_out=small[:, 8 + 2 * c + b:9 + 2 * c + b])
                    ins.then_inc(stat_ready, 1)
                    for b in range(3):
                        act.wait_ge(turned, t.after(turned))
                        for k in range(2 * b, min(2 * b + 2, 5)):
                            ins = act.activation(act_hi[:, k, :], ps[:, 4 + b, (k % 2) * T:(k % 2) * T + T],
                                                 ACT.Copy, scale=cst[:, G_MLA + k:G_MLA + k + 1])
                        if b == 2:
                            ins = act.activation(area(M_KRT, T), ps[:, 6, T:2 * T], ACT.Copy)
                        ins.then_inc(turned_hi, 1)
                    split(2)
                    product_done()
                    for b in range(TB):
                        ins = act.activation(tok(M_QR, 512)[:, b, :], ps[:, b, :], ACT.Copy)
                    ins.then_inc(acc_kept, 1)
                    split(3)
                    product_done()
                    for b in range(4):
                        ins = act.activation(area(A_QT + 512 * b, 512), ps[:, 4 + b, :], ACT.Copy)
                    ins.then_inc(acc_kept, 1)
                    split(2)
                    product_done()
                    for b in range(4):
                        ins = act.activation(area(A_KT + 512 * b, 512), ps[:, b, :], ACT.Copy)
                    ins.then_inc(acc_kept, 1)
                    split(2)
                    keep_acc(v_tok, 1)
                    keep_turned(area(M_QRT, 1024), range(2))
                    attention(M_SM, M_PT)
                else:
                    relu = blk(S_RELU, 2, PAIR)

                    def relus(heads):
                        for h in heads:
                            act.wait_ge(i_done, t.after(i_done))
                            if h >= 2:
                                act.wait_ge(relu_used, t.after(relu_used))
                            act.activation(relu[:, h % 2, :], ps[:, 4 + h % 4, 0:PAIR],
                                           ACT.Relu).then_inc(relu_done, 1)

                    split(KD)
                    keep_acc(tok(S_I, 584), 0, 584)
                    split(4)
                    keep_turned(area(S_IT, 1024), range(2))
                    act.wait_ge(turned, t.after(turned))
                    act.activation(area(S_KIT, T), ps[:, 2, 0:T], ACT.Copy).then_inc(turned_kept, 1)
                    split(4)
                    keep_acc(q_tok, 1)
                    split(4)
                    relus(range(4))
                    split(2)
                    relus(range(4, H2))
                    t.skip(relu_used, 2)
                    split(2)
                    keep_acc(k_tok, 0)
                    split(KD)
                    keep_acc(v_tok, 1)
                    keep_turned(area(A_QT, 2048), range(4))
                    keep_turned(area(A_KT, 2048), range(4, 8))
                    attention(S_SM, S_PT)
                split(KD)
                layer_norm()

                turned_ln(2 * i)
                for n in range(2 * H2):
                    act.wait_ge(unit_used, t.value(unit_used) + 1)
                    act.activation(area(E_Q + T * n, T), ps[:, 4 + n % 4, 0:T], ACT.Copy).then_inc(work_kept, 1)
                    split()
                for r in range(8):
                    act.wait_ge(scores_done, t.after(scores_done))
                    act.activation(area(E_S + 512 * r, 512), ps[:, 4 + r % 4, :], ACT.Copy).then_inc(work_kept, 1)
                def activate(c, j):
                    act.wait_ge(unit_used, t.value(unit_used) + 1)
                    act.activation(keep[:, bass.ds(c, 1), :].rearrange("p a t -> p (a t)"),
                                   ps[:, 4 + j % 4, 0:T], ACT.Gelu).then_inc(work_kept, 1)
                    split()

                turn = PAIRS * SPREAD
                with t.loop(NK // turn, [(scores_taken, PAIRS)] + unit_steps(turn)) as n:
                    for j in range(turn):
                        if j == turn - 1:
                            act.wait_ge(scores_taken, t.after(scores_taken, PAIRS))
                        activate(n * turn + j, j)
                act.wait_ge(scores_taken, t.after(scores_taken))
                for j in range(SPREAD):
                    activate(NK - SPREAD + j, j)
                    if j == SPREAD - 3:
                        act.wait_ge(best_ready, t.after(best_ready))
                        act.activation(pad[:, X_G:X_G + T], pad[:, X_G:X_G + T], ACT.Exp).then_inc(gates_exp, 1)
                act.wait_ge(turned, t.after(turned))
                act.activation(hot[:, 0:2, :].rearrange("p a t -> p (a t)"), ps[:, 4, :], ACT.Copy).then_inc(hot_ready, 1)
                act.wait_ge(turned, t.after(turned))
                act.activation(hot[:, 2, :], ps[:, 5, 0:T], ACT.Copy).then_inc(hot_ready, 1)
                act.activation(hot[:, 3, :], ps[:, 5, 0:T], ACT.Copy, scale=-1.0).then_inc(hot_ready, 1)
                act.wait_ge(hot_ready, t.after(hot_ready, 3))

                def distances(q, s):
                    for j in range(4 - ACT_HOT, 4):
                        ins = act.activation(near[:, 4 * s + j, :], iota, ACT.Abs,
                                             bias=hot[:, 1, bass.ds(q * 4 + j, 1)], scale=-1.0)
                    ins.then_inc(act_step, 1)

                def one_hots(q, s):
                    for j in range(4 - ACT_HOT, 4):
                        ins = act.activation(second_hot[:, s, j, :], near[:, 4 * s + j, :], ACT.Relu,
                                             bias=hot[:, 2, bass.ds(q * 4 + j, 1)],
                                             scale=hot[:, 3, bass.ds(q * 4 + j, 1)])
                    ins.then_inc(hot3_done, 1)

                distances(0, 0)
                for s in range(HOT):
                    if s + 1 < HOT:
                        distances(s + 1, s + 1)
                    act.wait_ge(act_step, t.after(act_step))
                    one_hots(s, s)
                with t.loop(T // (4 * HOT) - 1, [(gates_done, HOT), (act_step, HOT), (hot3_done, HOT)]) as n:
                    act.wait_ge(hot3_done, t.after(hot3_done, HOT))
                    distances(n * HOT + HOT, 0)
                    for s in range(HOT):
                        if s + 1 < HOT:
                            distances(n * HOT + (HOT + s + 1), s + 1)
                        act.wait_ge(act_step, t.after(act_step))
                        act.wait_ge(gates_done, t.after(gates_done))
                        one_hots(n * HOT + (HOT + s), s)
                t.skip(hot3_done, HOT)
                t.skip(gates_done, HOT)
                act.wait_ge(gates_used, t.after(gates_used, T // 4))

                def chunk_high(c, j):
                    act.activation(act_hi[:, j, :], keep[:, bass.ds(c, 1), :].rearrange("p a t -> p (a t)"),
                                   ACT.Copy).then_inc(eh_hi, 1)

                for j in range(RING):
                    chunk_high(j, j)
                with t.loop(NK // TURN, unit_steps(TURN)) as n:
                    for j in range(TURN):
                        split()
                        chunk_high(n * TURN + (RING + j), j % RING)
                for j in range(NK % TURN - RING):
                    split()
                    chunk_high(NK - NK % TURN + RING + j, j % RING)
                split(RING)
                layer_norm()

        @block.vector
        def _(dve):
            t = Tally(dve)
            units = [0]

            def step(ins):
                ins.then_inc(dve_step, 1)
                dve.wait_ge(dve_step, t.after(dve_step))

            def split(n=1):
                for _ in range(n):
                    u = units[0]
                    units[0] += 1
                    dve.wait_ge(hi_done, t.after(hi_done))
                    dve.tensor_tensor(w_lo[:, u % RAW, :], raw[:, u % RAW, :],
                                      w_hi[:, u % SPLIT, :].bitcast(F32), ALU.subtract).then_inc(lo_done, 1)

            def product_done(pending=0):
                dve.wait_ge(unit_used, t.at[hi_done.name] + pending - SPLIT)

            def variance(b, at, eps):
                dve.wait_ge(stat_ready, t.after(stat_ready))
                dve.tensor_scalar(small[:, b:b + 1], small[:, at + b:at + b + 1], 1.0 / D, eps, ALU.mult,
                                  ALU.add).then_inc(var_ready, 1)

            def turned_low(gain=None):
                for b in range(4):
                    dve.wait_ge(turned_hi, t.after(turned_hi))
                    if gain is None:
                        ins = dve.tensor_tensor(act_lo[:, 2 * b:2 * b + 2, :].rearrange("p k t -> p (k t)"),
                                                ps[:, 4 + b, :],
                                                act_hi[:, 2 * b:2 * b + 2, :].rearrange("p k t -> p (k t)").bitcast(F32),
                                                ALU.subtract)
                    else:
                        for k in (2 * b, 2 * b + 1):
                            ins = low_with_gain(k, ps[:, 4 + b, (k % 2) * T:(k % 2) * T + T], gain)
                    ins.then_inc(act_ready, 1)

            def low_with_gain(k, src, gain):
                return dve.scalar_tensor_tensor(act_lo[:, k, :], src, cst[:, gain + k:gain + k + 1],
                                                act_hi[:, k, :].bitcast(F32), ALU.mult, ALU.subtract)

            def turned_ln():
                for b in range(4):
                    dve.wait_ge(turned_hi, t.after(turned_hi))
                    dve.tensor_tensor(act_lo[:, 2 * b:2 * b + 2, :], xT[:, 2 * b:2 * b + 2, :],
                                      act_hi[:, 2 * b:2 * b + 2, :].bitcast(F32), ALU.subtract).then_inc(act_ready, 1)

            def norm(g, pending=0, late=0):
                for b in range(TB):
                    variance(b, 8, EPS)
                    if b == 0 and pending == 1:
                        split()
                    dve.wait_ge(rstd_ready, t.after(rstd_ready))
                    dve.tensor_scalar(diag[:, b, :], ident, small[:, 16 + b:17 + b], None,
                                      ALU.mult).then_inc(rows_ready, 1)
                    if b < pending and pending > 1:
                        split()
                split(max(0, pending - TB) + late)
                turned_low(G_NORM + KD * g)

            def ffn():
                def chunk(s, units_after=2):
                    dve.wait_ge(silu_done, t.after(silu_done))
                    dve.tensor_tensor(prod[:, s, :], silu[:, s, :], ps[:, 4 + s, T:2 * T],
                                      ALU.mult).then_inc(h_ready, 1)
                    split()
                    dve.wait_ge(h_hi_ready, t.after(h_hi_ready))
                    dve.tensor_tensor(h_lo[:, s, :], prod[:, s, :], h_hi[:, s, :].bitcast(F32),
                                      ALU.subtract).then_inc(h_lo_ready, 1)
                    split(units_after)

                chunk(0)
                with t.loop(5, [(silu_done, 4), (h_hi_ready, 4), (hi_done, 12)]):
                    for j in range(4):
                        chunk((j + 1) % 2)
                chunk(1, 1)
                product_done(1)
                for b in range(TB):
                    dve.scalar_tensor_tensor(x[:, b, :], acc(0)[:, b, :], 0.5, x[:, b, :], ALU.mult,
                                             ALU.add).then_inc(x_ready, 1)

            def head_norm(rows, scale, eps):
                dve.wait_ge(acc_kept, t.after(acc_kept))
                flat = rows.rearrange("p b n -> p (b n)")
                sqf = sq.rearrange("p b n -> p (b n)")
                step(dve.tensor_tensor(sqf, flat, flat, ALU.mult))
                split()
                step(dve.tensor_reduce(small[:, 32:64], sqf.rearrange("p (h d) -> p h d", d=HD), AX_X, ALU.add))
                dve.tensor_scalar(small[:, 32:64], small[:, 32:64], scale, eps, ALU.mult,
                                  ALU.add).then_inc(var_ready, 1)
                split(4)
                dve.wait_ge(rstd_ready, t.after(rstd_ready))
                heads = flat.rearrange("p (h d) -> p h d", d=HD)
                dve.tensor_tensor(heads, heads, small[:, 64:96].unsqueeze(2).broadcast_to([P, 32, HD]),
                                  ALU.mult).then_inc(rows_ready, 1)
                split(KD - 5)

            def heads_low(k, bank):
                dve.wait_ge(o_hi, t.after(o_hi))
                dve.tensor_tensor(act_lo[:, k, :], ps[:, bank, 0:T], act_hi[:, k, :].bitcast(F32),
                                  ALU.subtract).then_inc(act_ready, 1)

            def stick_breaking():
                ln, soft = blk(A_LN, 8, PAIR), blk(A_SOFT, 4, PAIR)

                def log_weights(p):
                    dve.wait_ge(z_used, t.after(z_used))
                    dve.wait_ge(c_done, t.after(c_done))
                    w = logw[:, 2 * p:2 * p + 2, :]
                    dve.tensor_tensor(w, w, ps[:, 0:2, 0:PAIR], ALU.subtract).then_inc(c_used, 1)

                for p in range(N_PAIRS):
                    s, r = slice(2 * (p % 2), 2 * (p % 2) + 2), slice(2 * (p % 4), 2 * (p % 4) + 2)
                    z = ps[:, 2 + 2 * (p % 3):4 + 2 * (p % 3), 0:PAIR]
                    dve.wait_ge(ln_done, t.after(ln_done))
                    if p >= 2:
                        dve.wait_ge(stay_ready, t.after(stay_ready))
                    dve.scalar_tensor_tensor(soft[:, s, :], z, 0.0, ln[:, r, :], ALU.max,
                                             ALU.add).then_inc(soft_done, 1)
                    dve.scalar_tensor_tensor(logw[:, 2 * p:2 * p + 2, :], z, 0.0, ln[:, r, :], ALU.min,
                                             ALU.subtract).then_inc(z_used, 1)
                    if p >= 1:
                        log_weights(p - 1)
                t.skip(stay_ready, 2)
                log_weights(N_PAIRS - 1)
                for p in range(N_PAIRS):
                    heads_low(p, 4 + p % 4)

            def rope(dst, src, ra, rb, at, half):
                n, h = src.shape[1], src.shape[2]
                cos, sin = (area(a, TB * half).rearrange("p (b d) -> p b d", b=TB).unsqueeze(2)
                            .broadcast_to([P, TB, h, half]) for a in at)
                x1, x2 = src[:, :, :, 0:half], src[:, :, :, half:2 * half]
                a1, a2 = ra[:, :, :, 0:half], ra[:, :, :, half:2 * half]
                b1, b2 = rb[:, :, :, 0:half], rb[:, :, :, half:2 * half]
                dve.tensor_tensor(a1, x1, cos, ALU.mult)
                dve.tensor_tensor(b1, x2, sin, ALU.mult)
                dve.tensor_tensor(a2, x2, cos, ALU.mult)
                step(dve.tensor_tensor(b2, x1, sin, ALU.mult))
                dve.tensor_tensor(dst[:, :, :, 0:half], a1, b1, ALU.subtract)
                return dve.tensor_tensor(dst[:, :, :, half:2 * half], a2, b2, ALU.add)

            def heads_of(at, h, d, row=None, off=0):
                row = row or h * d
                return tok(at, row)[:, :, off:off + h * d].rearrange("p b (h d) -> p b h d", h=h)

            def attention(sm_at, mask, scale):
                sm = blk(sm_at, H2, PAIR)
                parts = ((0, P), (P, PAIR))
                for n in range(H2 + 3):
                    if n < H2:
                        dve.wait_ge(s_done, t.after(s_done))
                        ins = dve.scalar_tensor_tensor(sm[:, n, :], ps[:, n % 4, 0:PAIR], scale, mask,
                                                       ALU.mult, ALU.add)
                        ins.then_inc(s_used, 1)
                        dve.wait_ge(s_used, t.after(s_used))
                        for b, (lo, hi) in enumerate(parts):
                            ins = dve.tensor_reduce(stats[:, 2 * n + b:2 * n + b + 1], sm[:, n, lo:hi], AX_X,
                                                    ALU.max, negate=True)
                        ins.then_inc(max_ready, 1)
                    if 1 <= n <= H2:
                        m = n - 1
                        dve.wait_ge(e_done, t.after(e_done))
                        step(dve.reciprocal(stats[:, 32 + 2 * (m % 8):34 + 2 * (m % 8)], stats[:, 16 + 2 * m:18 + 2 * m]))
                        for b, (lo, hi) in enumerate(parts):
                            ins = dve.tensor_scalar(sm[:, m, lo:hi], sm[:, m, lo:hi],
                                                    stats[:, 32 + 2 * m + b:33 + 2 * m + b], None, ALU.mult)
                        ins.then_inc(p_ready, 1)
                    if n >= 3:
                        heads_low(n - 3, 6 + (n - 3) % 2)

            def layer_norm():
                product_done(1)
                for b in range(TB):
                    step(dve.scalar_tensor_tensor(x[:, b, :], x[:, b, :], ALPHA, acc(0)[:, b, :], ALU.mult,
                                                  ALU.add, accum_out=small[:, 8 + b:9 + b]))
                    dve.tensor_scalar(small[:, 12 + b:13 + b], small[:, 8 + b:9 + b], -1.0 / D, None,
                                      ALU.mult).then_inc(mean_ready, 1)
                dve.wait_ge(mean_ready, t.after(mean_ready, TB))
                for b in range(TB):
                    variance(b, 10, LN_EPS)
                    if b == 0:
                        split()
                    dve.wait_ge(rstd_ready, t.after(rstd_ready))
                    dve.tensor_scalar(x[:, b, :], x[:, b, :], small[:, 12 + b:13 + b], small[:, 16 + b:17 + b],
                                      ALU.add, ALU.mult).then_inc(rows_ready, 1)

            def finish_x():
                dve.wait_ge(ln_in, t.after(ln_in, 16))
                for b in range(TB):
                    xb = x[:, b, :]
                    step(dve.tensor_tensor(xb, xb, ln_g, ALU.mult))
                    dve.tensor_tensor(xb, xb, ln_b, ALU.add).then_inc(x_ready, 1)

            step(dve.memset(zero[:, :].bitcast(F32), 0.0))
            dve.wait_ge(consts_in, 16)
            for i in range(DEPTH):
                norm(4 * i, 3 * i, SPLIT * (1 - i))
                ffn()
                norm(4 * i + 1, 1)
                if i == 0:
                    split(KD)
                    head_norm(q_tok, 1.0, HD * EPS)
                    head_norm(k_tok, 1.0 / HD, EPS)
                    t.skip(acc_kept)
                    stick_breaking()
                    split(KD - 1)
                    product_done(1)
                    for b in range(TB):
                        dve.tensor_tensor(x[:, b, :], acc(0)[:, b, :], x[:, b, :], ALU.add).then_inc(x_ready, 1)
                else:
                    split(KD)
                    t.skip(acc_kept)
                    turned_low()
                    dve.wait_ge(pool_in, t.after(pool_in, 32))
                    product_done(2)
                    for b in range(TB):
                        step(dve.tensor_tensor(sq[:, b, :], acc(0)[:, b, :], area(A_SCALE, D), ALU.mult))
                        dve.tensor_tensor(x[:, b, :], sq[:, b, :], x[:, b, :], ALU.add).then_inc(x_ready, 1)
                norm(4 * i + 2, i + 1)
                ffn()
                norm(4 * i + 3, 1)
                split(KD)
                dve.wait_ge(acc_kept, t.after(acc_kept))
                product_done(3)
                for b in range(TB):
                    step(dve.tensor_tensor(sq[:, b, :], acc(1)[:, b, :], sigma[:, b, :], ALU.mult))
                    dve.tensor_tensor(x[:, b, :], sq[:, b, :], x[:, b, :], ALU.add).then_inc(x_ready, 1)
            split(3)
            for i in range(DEPTH):
                if i == 0:
                    turned_low()
                else:
                    turned_ln()
                    finish_x()
                if i == 0:
                    c_tok = tok(M_C, 704)
                    split(KD)
                    dve.wait_ge(acc_kept, t.after(acc_kept))
                    dve.wait_ge(rope_in, t.after(rope_in, 16))
                    tables = (M_ROPE, M_ROPE + 64)
                    krd = tok(M_KRD, P)
                    kr4 = lambda off: krd[:, :, off:off + ROPE].unsqueeze(2)
                    step(rope(kr4(0), heads_of(M_C, 1, ROPE, 704, 640), heads_of(M_RA, 1, ROPE),
                              heads_of(M_RB, 1, ROPE), tables, 32))
                    dve.tensor_copy(krd[:, :, ROPE:P], krd[:, :, 0:ROPE])
                    dve.wait_ge(stat_ready, t.after(stat_ready))
                    dve.tensor_scalar(small[:, 0:2], small[:, 8:10], 1.0 / Q_RANK, EPS, ALU.mult, ALU.add)
                    dve.tensor_scalar(small[:, 2:4], small[:, 10:12], 1.0 / KV_RANK, EPS, ALU.mult,
                                      ALU.add).then_inc(var_ready, 1)
                    dve.wait_ge(rstd_ready, t.after(rstd_ready))
                    for c, (lo, hi) in enumerate(((0, Q_RANK), (Q_RANK, Q_RANK + KV_RANK))):
                        for b in range(TB):
                            ins = dve.tensor_scalar(c_tok[:, b, lo:hi], c_tok[:, b, lo:hi],
                                                    small[:, 16 + 2 * c + b:17 + 2 * c + b], None, ALU.mult)
                    ins.then_inc(rows_ready, 1)
                    for b in range(3):
                        dve.wait_ge(turned_hi, t.after(turned_hi))
                        for k in range(2 * b, min(2 * b + 2, 5)):
                            ins = low_with_gain(k, ps[:, 4 + b, (k % 2) * T:(k % 2) * T + T], G_MLA)
                        ins.then_inc(act_ready, 1)
                    split(2)
                    dve.wait_ge(acc_kept, t.after(acc_kept))
                    rope(heads_of(M_ROT, H2, ROPE), heads_of(M_QR, H2, ROPE), heads_of(M_RA, H2, ROPE),
                         heads_of(M_RB, H2, ROPE), tables, 32).then_inc(rows_ready, 1)
                    split(3)
                    split(2)
                    split(2)
                    t.skip(acc_kept, 3)
                    attention(M_SM, area(M_ROPE + 128, PAIR), (P + ROPE) ** -0.5)
                else:
                    split(KD)
                    dve.wait_ge(acc_kept, t.after(acc_kept))
                    dve.wait_ge(rope_in, t.after(rope_in, 16))
                    tables = (S_ROPE, S_ROPE + 64)
                    wide = (S_ROPE + 512, S_ROPE + 640)
                    i_tok = tok(S_I, 584)
                    kid = tok(S_KID, P)
                    rope(heads_of(S_IROT, H2, IDX), heads_of(S_I, H2, IDX, 584), heads_of(S_RA, H2, IDX),
                         heads_of(S_RB, H2, IDX), tables, 32)
                    step(rope(kid[:, :, 0:IDX].unsqueeze(2), heads_of(S_I, 1, IDX, 584, 512),
                              heads_of(S_RA + 1024, 1, IDX), heads_of(S_RB + 1024, 1, IDX), tables, 32))
                    dve.tensor_scalar(i_tok[:, :, 576:584], i_tok[:, :, 576:584], (H2 * IDX) ** -0.5, None, ALU.mult)
                    dve.tensor_copy(kid[:, :, IDX:P], kid[:, :, 0:IDX]).then_inc(rows_ready, 1)
                    split(KD)
                    dve.wait_ge(acc_kept, t.after(acc_kept))
                    rope(heads_of(S_QROT, H2, P), heads_of(A_Q, H2, P), heads_of(S_RA, H2, P),
                         heads_of(S_RB, H2, P), wide, 64).then_inc(rows_ready, 1)
                    relu, score = blk(S_RELU, 2, PAIR), area(S_IDX, PAIR)

                    def index_score(heads):
                        for h in heads:
                            dve.wait_ge(relu_done, t.after(relu_done))
                            for b, (lo, hi) in enumerate(((0, P), (P, PAIR))):
                                w = i_tok[:, b, 576 + h:577 + h]
                                r = relu[:, h % 2, lo:hi]
                                if h == 0:
                                    ins = dve.tensor_scalar(score[:, lo:hi], r, w, None, ALU.mult)
                                else:
                                    ins = dve.scalar_tensor_tensor(score[:, lo:hi], r, w, score[:, lo:hi],
                                                                   ALU.mult, ALU.add)
                            ins.then_inc(relu_used, 1)
                            dve.wait_ge(relu_used, t.after(relu_used))

                    split(4)
                    index_score(range(4))
                    split(2)
                    index_score(range(4, H2))
                    split(2)
                    work, sel = area(S_W, PAIR), area(S_SEL, PAIR)
                    step(dve.tensor_tensor(work, score, area(S_ROPE + 128, PAIR), ALU.add))
                    dve.wait_ge(acc_kept, t.after(acc_kept))
                    rope(heads_of(S_KROT, H2, P), heads_of(A_K, H2, P), heads_of(S_RA, H2, P),
                         heads_of(S_RB, H2, P), wide, 64).then_inc(rows_ready, 1)
                    for n in range(KEEP // 8):
                        if n < KD:
                            split()
                        dve.max(rank[:, 0:8], work[:, 0:P])
                        step(dve.max(rank[:, 8:16], work[:, P:PAIR]))
                        dve.match_replace(work[:, 0:P], rank[:, 0:8], work[:, 0:P], TAKEN)
                        step(dve.match_replace(work[:, P:PAIR], rank[:, 8:16], work[:, P:PAIR], TAKEN))
                    split(max(0, KD - KEEP // 8))
                    t.skip(acc_kept)
                    step(dve.tensor_scalar(sel, work, TAKEN / 2, NEG, ALU.is_gt, ALU.mult))
                    attention(S_SM, sel, P ** -0.5)
                split(KD - 1)
                layer_norm()

                turned_ln()
                finish_x()
                split(2 * H2)
                p0, p1 = pad[:, X_P0:X_P0 + T], pad[:, X_P1:X_P1 + T]
                ca, cb = pad[:, X_CA:X_CA + T], pad[:, X_CB:X_CB + T]
                eq = pad[:, X_P0:X_P0 + 2 * T].rearrange("p (k a) -> p k a", a=K16)
                val, best, idx_f, ab_f = rank[:, 0:32], rank[:, 32:48], rank[:, 48:80], rank[:, 80:112]
                idx_u, pos, ab_u = rank_u[:, 0:32], rank_u[:, 32:48], rank_u[:, 48:80]
                grid = lambda a: a.rearrange("p (a b) -> p a b", a=K16)
                row16 = lambda a: a.unsqueeze(1).broadcast_to([P, K16, K16])
                col16 = lambda a: a.unsqueeze(2).broadcast_to([P, K16, K16])
                i16 = cst[:, IOTA:IOTA + K16]

                def take(n):
                    dve.tensor_copy(p0, arena[:, bass.ds(n * T + E_S, T)]).then_inc(scores_taken, 1)
                    dve.wait_ge(scores_taken, t.after(scores_taken))

                def first8(n):
                    for f in range(2):
                        ins = dve.max(val[:, 16 * f:16 * f + 8], p0[:, NK * f:NK * f + NK])
                    step(ins)

                def first8_at(n):
                    for f in range(2):
                        v, row = val[:, 16 * f:16 * f + 8], slice(NK * f, NK * f + NK)
                        dve.max_index(idx_u[:, 16 * f:16 * f + 8], v, p0[:, row])
                        ins = dve.match_replace(p1[:, row], v, p0[:, row], TAKEN)
                    step(ins)

                def second8(n):
                    for f in range(2):
                        ins = dve.max(val[:, 16 * f + 8:16 * f + 16], p1[:, NK * f:NK * f + NK])
                    step(ins)

                def second8_at(n):
                    for f in range(2):
                        v, row = val[:, 16 * f + 8:16 * f + 16], slice(NK * f, NK * f + NK)
                        ins = dve.max_index(idx_u[:, 16 * f + 8:16 * f + 16], v, p1[:, row])
                    step(ins)
                    step(dve.tensor_tensor(grid(ca), col16(val[:, 0:16]), row16(val[:, 16:32]), ALU.add))

                def best8(n):
                    step(dve.max(best[:, 0:8], ca))
                    dve.tensor_copy(idx_f, idx_u)
                    dve.max_index(pos[:, 0:8], best[:, 0:8], ca)
                    step(dve.match_replace(cb, best[:, 0:8], ca, TAKEN))

                def best16(n):
                    step(dve.max(best[:, 8:16], cb))
                    dve.tensor_copy(pad[:, bass.ds(n * K16 + X_G, K16)], best)
                    step(dve.max_index(pos[:, 8:16], best[:, 8:16], cb))
                    dve.tensor_scalar(ab_u[:, 0:16], pos, 4, None, ALU.logical_shift_right)
                    step(dve.tensor_scalar(ab_u[:, 16:32], pos, 15, None, ALU.bitwise_and))
                    step(dve.tensor_copy(ab_f, ab_u))

                def decode(n):
                    step(dve.tensor_tensor(eq, i16.unsqueeze(1).broadcast_to([P, 2 * K16, K16]),
                                           ab_f.unsqueeze(2).broadcast_to([P, 2 * K16, K16]), ALU.is_equal))
                    for f in range(2):
                        half = eq[:, K16 * f:K16 * f + K16, :]
                        ins = dve.tensor_tensor(half, half, row16(idx_f[:, K16 * f:K16 * f + K16]), ALU.mult)
                    step(ins)
                    step(dve.tensor_reduce(pad[:, X_I1:X_I1 + 2 * T].rearrange("p (f t) -> p f t", f=2)
                                           [:, :, bass.ds(n * K16, K16)],
                                           eq.rearrange("p (f k) a -> p f k a", f=2), AX_X, ALU.add))

                dve.wait_ge(work_kept, t.after(work_kept, 2 * H2 + 8))
                t.skip(work_kept, NK)
                pieces = [first8, first8_at, second8, second8_at, best8, best16, decode]

                def pair(n):
                    take(n)
                    for j in range(SPREAD):
                        split()
                        if j < len(pieces):
                            pieces[j](n)

                with t.loop(NK // (PAIRS * SPREAD), [(hi_done, PAIRS * SPREAD), (scores_taken, PAIRS),
                                                     (dve_step, PAIRS * TOPK_STEPS)]) as n:
                    for p in range(PAIRS):
                        pair(n * PAIRS + p)
                take(TB * H2 - 1)
                for j in range(SPREAD // 2):
                    split()
                    for piece in pieces[2 * j:2 * j + 2]:
                        piece(TB * H2 - 1)
                g3 = pad[:, X_G:X_G + T].rearrange("p (n k) -> p n k", k=K16)
                step(dve.tensor_copy(small[:, 32:48], g3[:, :, 0]))
                dve.tensor_tensor(g3, g3, small[:, 32:48].unsqueeze(2).broadcast_to([P, K16, K16]),
                                  ALU.subtract).then_inc(best_ready, 1)
                split(2)
                dve.wait_ge(gates_exp, t.after(gates_exp))
                step(dve.tensor_reduce(small[:, 48:64], g3, AX_X, ALU.add))
                step(dve.reciprocal(small[:, 64:80], small[:, 48:64]))
                dve.tensor_tensor(g3, g3, small[:, 64:80].unsqueeze(2).broadcast_to([P, K16, K16]),
                                  ALU.mult).then_inc(ranks_ready, 1)
                split(SPREAD // 2 - 2)
                dve.wait_ge(hot_ready, t.after(hot_ready, 3))

                def one_hots(q, s):
                    for j in range(POOL_HOT, 4):
                        dve.tensor_scalar(first_hot[:, s, j, :], iota, hot[:, 0, bass.ds(q * 4 + j, 1)], None,
                                          ALU.is_equal)
                    for j in range(4 - ACT_HOT):
                        ins = dve.tensor_scalar(second_hot[:, s, j, :], iota,
                                                hot[:, 1, bass.ds(q * 4 + j, 1)], hot[:, 2, bass.ds(q * 4 + j, 1)],
                                                ALU.is_equal, ALU.mult)
                    ins.then_inc(hot2_done, 1)

                def use_gates(q, s):
                    dve.wait_ge(gates_done, t.after(gates_done))
                    cols = keep[:, :, bass.ds(q * 4, 4)].rearrange("p c t -> p t c")
                    dve.tensor_tensor(cols, ps[:, 4 + s, :].rearrange("p (t c) -> p t c", t=4), cols,
                                      ALU.mult).then_inc(gates_used, 1)

                for s in range(HOT):
                    one_hots(s, s)
                with t.loop(T // (4 * HOT) - 1, [(gates_done, HOT)]) as n:
                    for s in range(HOT):
                        use_gates(n * HOT + s, s)
                        one_hots(n * HOT + (HOT + s), s)
                for s in range(HOT):
                    use_gates(T // 4 - HOT + s, s)
                dve.wait_ge(gates_used, t.after(gates_used, T // 4))

                def chunk_low(c, j):
                    dve.wait_ge(eh_hi, t.after(eh_hi))
                    dve.tensor_tensor(act_lo[:, j, :], keep[:, bass.ds(c, 1), :].rearrange("p a t -> p (a t)"),
                                      act_hi[:, j, :].bitcast(F32), ALU.subtract).then_inc(eh_ready, 1)

                for j in range(RING):
                    chunk_low(j, j)
                with t.loop(NK // TURN, [(hi_done, TURN), (eh_hi, TURN)]) as n:
                    for j in range(TURN):
                        split()
                        chunk_low(n * TURN + (RING + j), j % RING)
                for j in range(NK % TURN - RING):
                    split()
                    chunk_low(NK - NK % TURN + RING + j, j % RING)
                split(RING - 1)
                layer_norm()
            finish_x()

        @block.tensor
        def _(pe):
            t = Tally(pe)
            units = [0]

            def unit():
                pe.wait_ge(lo_done, t.after(lo_done))
                units[0] += 1
                return units[0] - 1

            def mm3(dst, lhs, rhs, first, last, **kw):
                pe.matmul(dst, lhs[0], rhs[0], start=first, stop=False, **kw)
                pe.matmul(dst, lhs[0], rhs[1], start=False, stop=False, **kw)
                return pe.matmul(dst, lhs[1], rhs[0], start=False, stop=last, **kw)

            def w(s, lo, n):
                return w_hi[:, s % SPLIT, lo:lo + n], w_lo[:, s % RAW, lo:lo + n]

            def a(k, lo=0, n=T):
                return act_hi[:, k, lo:lo + n], act_lo[:, k, lo:lo + n]

            def rows(set_, n_units, n=D, fresh=True, at=0, then={}):
                for k in range(n_units):
                    if fresh and k % 2 == 0:
                        pe.wait_ge(act_ready, t.after(act_ready))
                    s = unit()
                    for b in range(TB):
                        lhs = a(at + k, P * b, P)
                        for lo in range(0, n, 512):
                            m = min(512, n - lo)
                            ins = mm3(ps[:, 4 * set_ + 2 * b + lo // 512, 0:m], lhs, w(s, lo, m), k == 0,
                                      k == n_units - 1)
                    ins.then_inc(unit_used, 1)
                    if k in then:
                        then[k]()

            def turn(blocks, bank):
                for n, src in enumerate(blocks):
                    for b in range(TB):
                        ins = pe.transpose(ps[:, bank, T * n + P * b:T * n + P * b + P], src[:, b, :], ident)
                ins.then_inc(turned, 1)

            def turn_rows(src, banks):
                for n, bank in enumerate(banks):
                    turn([src[:, :, P * k:P * k + P] for k in (2 * n, 2 * n + 1)], bank)

            def turn_x(product=False):
                for b in range(TB):
                    pe.wait_ge(rows_ready, t.after(rows_ready))
                    for k in range(KD):
                        dst = ps[:, 4 + k // 2, T * (k % 2) + P * b:T * (k % 2) + P * b + P]
                        src = x[:, b, P * k:P * k + P]
                        if product:
                            ins = pe.matmul(dst, src, diag[:, b, :], start=True, stop=True)
                        else:
                            ins = pe.transpose(dst, src, ident)
                        if b == TB - 1 and k % 2:
                            ins.then_inc(turned, 1)

            def norm():
                turn_x(True)

            def open_acc():
                for b in range(4):
                    pe.matmul(ps[:, b, :], zero[0:1, :], zero[0:1, :].unsqueeze(1).broadcast_to([1, 4, P]),
                              start=True, stop=False, skip_group_check=True)

            def ffn():
                def features(dst, fresh=False):
                    s = unit()
                    for k in range(KD):
                        if fresh and k % 2 == 0:
                            pe.wait_ge(act_ready, t.after(act_ready))
                        ins = mm3(dst, w(s, P * k, P), a(k), k == 0, k == KD - 1)
                    return ins

                def gate_up(s, fresh=False):
                    features(ps[:, 4 + s, 0:T], fresh).then_inc(unit_used, 1)
                    features(ps[:, 4 + s, T:2 * T]).then_inc(unit_used, 1)

                def down(s, last=False):
                    pe.wait_ge(h_lo_ready, t.after(h_lo_ready))
                    slot = unit()
                    for b in range(TB):
                        lhs = h_hi[:, s, P * b:P * b + P], h_lo[:, s, P * b:P * b + P]
                        for half in range(2):
                            ins = mm3(ps[:, 2 * b + half, :], lhs, w(slot, 512 * half, 512), False, last,
                                      skip_group_check=True)
                    ins.then_inc(unit_used, 1)

                gate_up(0, True)
                open_acc()
                with t.loop(5, [(lo_done, 12), (h_lo_ready, 4)]):
                    for j in range(4):
                        gate_up((j + 1) % 2)
                        down(j % 2)
                gate_up(1)
                down(0)
                down(1, True)

            def stick_breaking():
                mask_tri = area(A_STICKC + PAIR, P)
                ones = area(A_STICKC + PAIR + P, P)
                pe.wait_ge(turned_kept, t.after(turned_kept, 8))
                pe.wait_ge(stick_in, 16)

                def scores(p):
                    if p >= 3:
                        pe.wait_ge(z_used, t.after(z_used))
                    for h in range(2):
                        z, r = ps[:, 2 + 2 * (p % 3) + h, :], slice(64 * h, 64 * h + 64)
                        pe.matmul(z[:, 0:T], kT[r, p, 0:P], qT[r, p, 0:T], start=True, stop=True)
                        ins = pe.matmul(z[:, T:PAIR], kT[r, p, P:T], qT[r, p, P:T], start=True, stop=True)
                    ins.then_inc(z_done, 1)

                for p in range(3):
                    scores(p)
                for p in range(N_PAIRS):
                    if p + 3 < N_PAIRS:
                        scores(p + 3)
                    pe.wait_ge(stay_ready, t.after(stay_ready))
                    if p >= 1:
                        pe.wait_ge(c_used, t.after(c_used))
                    for h in range(2):
                        c, s = ps[:, h, :], stay[:, 2 * p + h, :]
                        pe.matmul(c[:, 0:PAIR], mask_tri, s, start=True, stop=False)
                        ins = pe.matmul(c[:, P:T], ones, s[:, T:PAIR], start=False, stop=True)
                    ins.then_inc(c_done, 1)
                t.skip(c_used)
                pe.wait_ge(z_used, t.after(z_used, 3))
                for p in range(N_PAIRS):
                    pe.wait_ge(w_ready, t.after(w_ready))
                    if p >= 4:
                        pe.wait_ge(act_ready, t.after(act_ready))
                    for h in range(2):
                        o, e = ps[64 * h:64 * h + 64, 4 + p % 4, :], logw[:, 2 * p + h, :]
                        v = slice(HD * (2 * p + h), HD * (2 * p + h) + HD)
                        pe.matmul(o[:, 0:T], v_tok[:, 0, v], e[:, 0:T], start=True, stop=False)
                        ins = pe.matmul(o[:, P:T], v_tok[:, 1, v], e[:, T:PAIR], start=False, stop=True)
                    ins.then_inc(o_done, 1)
                pe.wait_ge(act_ready, t.after(act_ready, 4))

            def attention(sm_at, pt_at, terms):
                sm, pT = blk(sm_at, H2, PAIR), blk(pt_at, H2, PAIR)

                def scores(h):
                    if h >= 4:
                        pe.wait_ge(s_used, t.after(s_used))
                    s, both = ps[:, h % 4, :], terms(h)
                    for lo, q0, keys in ((0, 0, P), (P, P, T)):
                        for n, (k, q) in enumerate(both):
                            ins = pe.matmul(s[:, lo:lo + keys], q[:, q0:q0 + P], k[:, 0:keys], start=n == 0,
                                            stop=n == len(both) - 1)
                    ins.then_inc(s_done, 1)

                for h in range(4):
                    scores(h)
                for n in range(1, H2 + 2):
                    if n <= H2:
                        h = n - 1
                        pe.wait_ge(p_ready, t.after(p_ready))
                        if h >= 2:
                            pe.wait_ge(p_kept, t.after(p_kept))
                        for c in range(3):
                            ins = pe.transpose(ps[:, 4 + h % 2, P * c:P * c + P],
                                               sm[:, h, P * c:P * c + P], ident)
                        ins.then_inc(p_turned, 1)
                    if n >= 2:
                        h = n - 2
                        if h == 0 or h == H2 - 1:
                            pe.wait_ge(p_kept, t.after(p_kept))
                        if h >= 2:
                            pe.wait_ge(act_ready, t.after(act_ready))
                        o, v = ps[:, 6 + h % 2, :], slice(P * h, P * h + P)
                        pe.matmul(o[:, 0:T], v_tok[:, 0, v], pT[:, h, 0:T], start=True, stop=False)
                        pe.matmul(o[:, P:T], v_tok[:, 1, v], pT[:, h, T:PAIR], start=False,
                                  stop=True).then_inc(o_done, 1)
                    if n + 3 < H2:
                        scores(n + 3)
                t.skip(s_used, 4)
                pe.wait_ge(act_ready, t.after(act_ready, 2))

            pe.wait_ge(consts_in, 16)
            for i in range(DEPTH):
                norm()
                ffn()
                norm()
                if i == 0:
                    rows(0, KD)
                    rows(1, KD, fresh=False)
                    pe.wait_ge(acc_kept, t.after(acc_kept))
                    rows(0, KD, fresh=False)
                    pe.wait_ge(acc_kept, t.after(acc_kept))
                    pe.wait_ge(rows_ready, t.after(rows_ready))
                    turn_rows(q_tok, range(4, 8))
                    pe.wait_ge(acc_kept, t.after(acc_kept))
                    pe.wait_ge(rows_ready, t.after(rows_ready))
                    turn_rows(k_tok, range(4))
                    stick_breaking()
                    rows(0, KD, fresh=False)
                else:
                    rows(0, KD)
                    pe.wait_ge(acc_kept, t.after(acc_kept))
                    pe.wait_ge(pool_in, t.after(pool_in, 32))
                    mats = area(A_POOLC, 2048).rearrange("p (g b t) -> p g b t", g=4, b=TB)
                    for bank in range(4):
                        for n in range(2):
                            c = slice(P * (2 * bank + n), P * (2 * bank + n) + P)
                            dst = ps[:, 4 + bank, T * n:T * n + T]
                            pe.matmul(dst, q_tok[:, 0, c], mats[:, bank, 0, :], start=True, stop=False)
                            ins = pe.matmul(dst[:, P:T], q_tok[:, 1, c], mats[:, bank, 1, P:T], start=False,
                                            stop=True)
                        ins.then_inc(turned, 1)
                    pe.wait_ge(act_ready, t.after(act_ready, 4))
                    s0, s1 = unit(), unit()
                    for b in range(TB):
                        for g in range(4):
                            dst = ps[:, 2 * b + g // 2, T * (g % 2):T * (g % 2) + T]
                            mm3(dst, a(2 * g, P * b, P), w(s0, T * g, T), True, False)
                            ins = mm3(dst, a(2 * g + 1, P * b, P), w(s1, T * g, T), False, True)
                    ins.then_inc(unit_used, 2)
                norm()
                ffn()
                norm()
                rows(0, KD)
                sp_, s0, s1 = unit(), unit(), unit()
                for n, s in enumerate((s0, s1)):
                    for b in range(TB):
                        lhs = w(sp_, T * n + P * b, P)
                        for half in range(2):
                            ins = mm3(ps[:, 4 + 2 * b + half, :], lhs, w(s, 512 * half, 512), n == 0, n == 1)
                ins.then_inc(unit_used, 3)
                t.skip(acc_kept)
            t.skip(x_ready, TB * (4 * DEPTH - 1))
            for i in range(DEPTH):
                if i == 0:
                    pe.wait_ge(x_ready, t.after(x_ready, TB))
                    turn_rows(x, range(4, 8))
                else:
                    turn_x()
                if i == 0:
                    c_tok, krd = tok(M_C, 704), tok(M_KRD, P)
                    rows(0, KD, 704)
                    pe.wait_ge(rows_ready, t.after(rows_ready))
                    c = [c_tok[:, :, P * k:P * k + P] for k in range(5)] + [krd]
                    for b in range(3):
                        turn(c[2 * b:2 * b + 2], 4 + b)
                    pe.wait_ge(act_ready, t.after(act_ready, 3))
                    s = unit()
                    for b in range(TB):
                        mm3(ps[:, b, :], a(0, P * b, P), w(s, 0, 512), True, False)
                        ins = mm3(ps[:, b, :], a(1, P * b, P), w(s, 512, 512), False, False)
                    ins.then_inc(unit_used, 1)
                    s = unit()
                    for b in range(TB):
                        ins = mm3(ps[:, b, :], a(2, P * b, P), w(s, 0, 512), False, True)
                    ins.then_inc(unit_used, 1)

                    def head_features(first_bank, depth, at):
                        for n in range(H2 * depth):
                            if n % 8 == 0:
                                if n:
                                    ins.then_inc(unit_used, 1)
                                s = unit()
                            h, r = divmod(n, depth)
                            ins = mm3(ps[:, first_bank + h // 2, T * (h % 2):T * (h % 2) + T],
                                      w(s, P * (n % 8), P), a(at + r), r == 0, r == depth - 1)
                        ins.then_inc(unit_used, 1)

                    head_features(4, 3, 0)
                    pe.wait_ge(acc_kept, t.after(acc_kept, 2))
                    head_features(0, 2, 3)
                    pe.wait_ge(acc_kept, t.after(acc_kept))
                    rows(1, 2, fresh=False, at=3)
                    pe.wait_ge(acc_kept, t.after(acc_kept))
                    pe.wait_ge(rows_ready, t.after(rows_ready))
                    turn_rows(tok(M_ROT, 512), range(2))
                    pe.wait_ge(turned_kept, t.after(turned_kept, 2))
                    pe.wait_ge(acc_kept, t.after(acc_kept))
                    qrT, krT = blk(M_QRT, 4), area(M_KRT, T)

                    def terms(h):
                        r = slice(64 * (h % 2), 64 * (h % 2) + 64)
                        return (kT[:, h, :], qT[:, h, :]), (krT[r, :], qrT[r, h // 2, :])

                    attention(M_SM, M_PT, terms)
                else:
                    qiT, kiT = blk(S_IT, 4), area(S_KIT, T)

                    def turn_indexer():
                        pe.wait_ge(acc_kept, t.after(acc_kept))
                        pe.wait_ge(rows_ready, t.after(rows_ready))
                        turn_rows(tok(S_IROT, 512), range(2))
                        turn([tok(S_KID, P)], 2)

                    def logits(heads):
                        for h in heads:
                            if h >= 4:
                                pe.wait_ge(relu_done, t.after(relu_done))
                            r = slice(64 * (h % 2), 64 * (h % 2) + 64)
                            for lo, q0, keys in ((0, 0, P), (P, P, T)):
                                ins = pe.matmul(ps[:, 4 + h % 4, lo:lo + keys], qiT[r, h // 2, q0:q0 + P],
                                                kiT[r, 0:keys], start=True, stop=True)
                            ins.then_inc(i_done, 1)

                    def first_logits():
                        pe.wait_ge(acc_kept, t.after(acc_kept))
                        logits(range(4))

                    rows(0, KD, 584)
                    rows(1, KD, fresh=False, then={3: turn_indexer})
                    pe.wait_ge(turned_kept, t.after(turned_kept, 3))
                    rows(0, KD, fresh=False, then={3: first_logits, 5: lambda: logits(range(4, H2))})
                    pe.wait_ge(relu_done, t.after(relu_done, 4))
                    rows(1, KD, fresh=False)
                    pe.wait_ge(acc_kept, t.after(acc_kept))
                    pe.wait_ge(rows_ready, t.after(rows_ready))
                    turn_rows(tok(S_QROT, D), range(4))
                    pe.wait_ge(acc_kept, t.after(acc_kept))
                    pe.wait_ge(rows_ready, t.after(rows_ready))
                    turn_rows(tok(S_KROT, D), range(4, 8))
                    pe.wait_ge(turned_kept, t.after(turned_kept, 8))
                    attention(S_SM, S_PT, lambda h: ((kT[:, h, :], qT[:, h, :]),))
                rows(0, KD, fresh=False)

                turn_x()

                def expert_features(bank, fresh=False):
                    s = unit()
                    for k in range(KD):
                        if fresh and k % 2 == 0:
                            pe.wait_ge(act_ready, t.after(act_ready))
                        ins = mm3(ps[:, 4 + bank, 0:T], w(s, P * k, P), a(k), k == 0, k == KD - 1)
                    ins.then_inc(unit_used, 1)

                for n in range(2 * H2):
                    if n >= 4:
                        pe.wait_ge(work_kept, t.after(work_kept))
                    expert_features(n % 4, n == 0)
                pe.wait_ge(work_kept, t.after(work_kept, 4))
                pe.wait_ge(subkeys_in, t.after(subkeys_in, 16))
                queries, keys = blk(E_Q, 16), blk(E_SK, 16, NK)
                for r in range(8):
                    if r >= 4:
                        pe.wait_ge(work_kept, t.after(work_kept))
                    for n in range(4):
                        hh = 4 * (r % 4) + n
                        ins = pe.matmul(ps[:, 4 + r % 4, NK * n:NK * n + NK], queries[:, hh, P * (r // 4):P * (r // 4) + P],
                                        keys[:, hh, :], start=True, stop=True)
                    ins.then_inc(scores_done, 1)
                with t.loop(NK // TURN, [(lo_done, TURN), (work_kept, TURN)]):
                    for j in range(TURN):
                        pe.wait_ge(work_kept, t.after(work_kept))
                        expert_features(j % 4)
                for j in range(NK % TURN):
                    pe.wait_ge(work_kept, t.after(work_kept))
                    expert_features(j % 4)
                pe.wait_ge(work_kept, t.after(work_kept, 4))
                pe.wait_ge(ranks_ready, t.after(ranks_ready))
                ranks = pad[:, X_I1:X_I1 + 3 * T].rearrange("p (n b c) -> p n b c", n=3, b=TB)
                turn([ranks[:, 0], ranks[:, 1]], 4)
                turn([ranks[:, 2]], 5)

                def gate_matrices(s):
                    pe.wait_ge(hot1_done, t.after(hot1_done))
                    pe.wait_ge(hot2_done, t.after(hot2_done))
                    pe.wait_ge(hot3_done, t.after(hot3_done))
                    for j in range(4):
                        ins = pe.matmul(ps[:, 4 + s, NK * j:NK * j + NK], first_hot[:, s, j, :],
                                        second_hot[:, s, j, :], start=True, stop=True)
                    ins.then_inc(gates_done, 1)

                for s in range(HOT):
                    gate_matrices(s)
                with t.loop(T // (4 * HOT) - 1, [(hot1_done, HOT), (hot2_done, HOT), (hot3_done, HOT),
                                                 (gates_used, HOT)]):
                    for s in range(HOT):
                        pe.wait_ge(gates_used, t.after(gates_used))
                        gate_matrices(s)
                pe.wait_ge(gates_used, t.after(gates_used, HOT))

                open_acc()

                def expert_down(j, last=False):
                    pe.wait_ge(eh_ready, t.after(eh_ready))
                    s = unit()
                    for b in range(TB):
                        for half in range(2):
                            ins = mm3(ps[:, 2 * b + half, :], a(j, P * b, P), w(s, 512 * half, 512), False, last,
                                      skip_group_check=True)
                    ins.then_inc(unit_used, 1)

                with t.loop(NK // TURN, [(lo_done, TURN), (eh_ready, TURN)]):
                    for j in range(TURN):
                        expert_down(j % RING)
                for j in range(NK % TURN):
                    expert_down(j % RING, j == NK % TURN - 1)


def _columns(w, chunk=P):
    k, n = w.shape
    return w.reshape(k // P, P, n // chunk, chunk).transpose(2, 1, 0, 3).reshape(n // chunk, P, -1)


def _blocks(w):
    return w.reshape(-1, P, w.shape[1])


def _padded(units):
    out = np.zeros(units.shape[:2] + (UNIT,), np.float32)
    out[:, :, :units.shape[2]] = units
    return out


def _heads(w, depth):
    a = w.reshape(depth, P, H2, P).transpose(1, 2, 0, 3).reshape(P, -1)
    return a.reshape(P, -1, UNIT).transpose(1, 0, 2)


def _stream(v):
    parts = []

    def ffn(gu, down):
        g, d = _columns(gu), _blocks(down)
        out = np.empty((3 * FC, P, UNIT), np.float32)
        order = [("g", 0), ("u", 0)]
        for c in range(1, FC):
            order += [("g", c), ("u", c), ("d", c - 1)]
        order += [("d", FC - 1)]
        for n, (kind, c) in enumerate(order):
            out[n] = g[c] if kind == "g" else g[FC + c] if kind == "u" else d[c]
        parts.append(out)

    for i in range(DEPTH):
        ffn(v["w_ffn1_gu"][i], v["w_ffn1_down"][i])
        if i == 0:
            qkv = v["w_qkv"][0]
            parts.extend(_blocks(qkv[:, D * n:D * n + D]) for n in range(3))
            parts.append(_blocks(v["w_o"][0]))
        else:
            parts.append(_blocks(v["w_pool_in"][0]))
            g = v["w_pool_grp"][0].reshape(4, 2, P, T)
            parts.append(g.transpose(1, 2, 0, 3).reshape(2, P, UNIT))
        ffn(v["w_ffn2_gu"][i], v["w_ffn2_down"][i])
        parts.append(_blocks(v["w_ple_gate"][i]))
        parts.append(_padded(v["p"][i, 0].T.reshape(2, P, T).transpose(1, 0, 2).reshape(1, P, 2 * T)))
        parts.append(_blocks(v["w_ple_proj"][i]))

    def peer(i):
        parts.append(_columns(v["peer_w_q_2"][i]))
        down = v["peer_w_down_2"][i].reshape(NK, NK, KD, P)
        parts.append(down.transpose(1, 3, 2, 0).reshape(NK, P, UNIT))
        parts.append(v["peer_w_up_2"][i].reshape(NK, NK, D).transpose(1, 0, 2))

    parts.append(_padded(_blocks(v["mla_w_in_2"][0])))
    uq, ukv = v["mla_w_uq_2"][0], v["mla_w_ukv_2"][0]
    rope = uq[:, :, P:].reshape(3, P, 512).transpose(1, 0, 2).reshape(P, 3 * 512)
    parts.append(rope[:, :UNIT][None])
    parts.append(_padded(rope[:, UNIT:][None]))
    parts.append(_heads(uq[:, :, :P], 3))
    parts.append(_heads(ukv[:, :, :P], 2))
    parts.append(_blocks(ukv[:, :, P:].reshape(KV_RANK, D)))
    parts.append(_blocks(v["mla_w_o_2"][0]))
    peer(0)
    w_in = v["dsa_w_in_2"][0]
    parts.append(_padded(_blocks(w_in[:, 3 * D:])))
    parts.extend(_blocks(w_in[:, D * n:D * n + D]) for n in range(3))
    parts.append(_blocks(v["dsa_w_o_2"][0]))
    peer(1)
    parts.append(np.zeros((N_UNITS - sum(len(a) for a in parts), P, UNIT), np.float32))
    return np.concatenate(parts)


def _consts(v):
    c = np.zeros((P, N_CONST), np.float32)
    c[:, IDENT:IDENT + P] = np.eye(P)
    c[:, IOTA:IOTA + P] = np.arange(P)
    c[:, HALF] = -0.5
    c[:, ONE] = 1.0
    c[:, QG] = np.tile(v["q_norm"][0], 2)
    c[:, KG] = np.tile(v["k_norm"][0], 2)
    c[:, G_MLA:G_MLA + 3] = v["mla_q_norm_2"][0].reshape(3, P).T
    c[:, G_MLA + 3:G_MLA + 5] = v["mla_kv_norm_2"][0].reshape(2, P).T
    for i in range(DEPTH):
        for n, name in enumerate(("norm_ffn1", "norm_mix", "norm_ffn2", "norm_ple")):
            at = G_NORM + KD * (4 * i + n)
            c[:, at:at + KD] = v[name][i].reshape(KD, P).T
    for n, name in enumerate(("ln_gain_2", "ln_bias_2")):
        for m in range(2 * DEPTH):
            at = G_LN + KD * (2 * m + n)
            c[:, at:at + KD] = v[name].reshape(2 * DEPTH, KD, P)[m].T
    return c


def _shape_tables():
    k, q = np.arange(P)[:, None], np.arange(T)[None, :]
    stick = np.zeros((P, STICK_COLS), np.float32)
    stick[:, 0:T] = k < q
    stick[:, T:PAIR] = k < q[:, :P]
    stick[:, PAIR:PAIR + P] = np.arange(P)[:, None] > np.arange(P)[None, :]
    stick[:, PAIR + P:] = 1.0
    pool = np.zeros((4, T, T), np.float32)
    for g, w in enumerate(WINDOWS):
        for s in range(T):
            n = min(s + 1, w)
            pool[g, s + 1 - n:s + 1, s] = np.float32(1.0) / np.float32(n)
            pool[g, s, s] -= 1.0
    pool = pool.reshape(4, TB, P, T).transpose(2, 0, 1, 3).reshape(P, -1)
    rope = np.zeros((P, ROPE_COLS), np.float32)
    for at, dim in ((0, ROPE), (512, P)):
        inv = np.float32(10000.0) ** (-np.arange(0, dim, 2, dtype=np.float32) / np.float32(dim))
        ang = np.arange(T, dtype=np.float32)[:, None] * inv[None, :].astype(np.float32)
        half = dim // 2
        for n, f in enumerate((np.cos, np.sin)):
            tab = f(ang).astype(np.float32).reshape(TB, P, half).transpose(1, 0, 2).reshape(P, TB * half)
            rope[:, at + n * TB * half:at + (n + 1) * TB * half] = tab
    chunk = np.arange(T) // 64
    mask = np.where(chunk[None, :] <= chunk[:, None], 0.0, NEG)
    rope[:, 128:256] = mask[0:P, 0:P]
    rope[:, 256:512] = mask[P:T, :]
    return stick, pool, rope


def kernel(**inputs):
    import concourse.bacc as bacc
    from concourse.bass_utils import run_bass_kernel_spmd

    v = {name: np.asarray(a) for name, a in inputs.items()}
    stick, pool, rope = _shape_tables()
    ln = np.stack([v["ln_gain_2"], v["ln_bias_2"]], axis=2).reshape(2 * DEPTH, 1, 2 * D)
    arrays = {
        "stream": _stream(v),
        "x": np.ascontiguousarray(v["x"][0]),
        "consts": _consts(v),
        "stick": stick,
        "pool": pool,
        "scale": np.ascontiguousarray(np.broadcast_to(v["pool_scale"], (P, D))),
        "rope": rope,
        "ln": np.ascontiguousarray(np.broadcast_to(ln, (2 * DEPTH, P, 2 * D))),
        "subkeys": np.ascontiguousarray(
            v["peer_sub_keys_2"].transpose(0, 4, 2, 1, 3).reshape(DEPTH, P, 2048)),
    }
    nc = bacc.Bacc("TRN2", target_bir_lowering=False, num_devices=1)
    args = [nc.dram_tensor(f"in_{name}", a.shape, mybir.dt.from_np(a.dtype), kind="ExternalInput").ap()
            for name, a in arrays.items()]
    out = nc.dram_tensor("out", (T, D), F32, kind="ExternalOutput").ap()
    program(nc, *args, out)
    r = run_bass_kernel_spmd(nc, [{f"in_{name}": a for name, a in arrays.items()}], core_ids=[0])
    return r.results[0]["out"].reshape(1, T, D)
```
